# Optimizing a Trainium2 kernel written in Bass

```python
import math
import jax, jax.numpy as jnp
from jax import lax
import numpy as np

D_MODEL = 1024
BATCH = 1
SEQ = 256
DEPTH = 1

RET_HEADS = 4
RET_DK = 128
RET_DV = 256
RET_CHUNK = 128
ROPE_BASE = 10000.0
ATT_PATTERNS = ((128, 1), (512, 4), (2048, 16))
ATT_GROUPS = 3
ATT_HEADS_PER_GROUP = 4
ATT_HEADS = ATT_GROUPS * ATT_HEADS_PER_GROUP
ATT_DH = 128
ATT_QBLOCK = 128
REL_BUCKETS = 32
REL_MAX_EXACT = REL_BUCKETS // 2
REL_MAX_DIST = 2048
N_EXPERTS = 32
TOP_K = 4
D_EXPERT = D_MODEL
SWIGLU_LIMIT = 7.0
SWIGLU_ALPHA = 1.702
MOE_BLOCK = 128
EPS = 1e-6
GN_EPS = 1e-5

RET_QK_W = RET_HEADS * RET_DK
RET_V_W = RET_HEADS * RET_DV
ATT_W = ATT_HEADS * ATT_DH
ATT_OUT_W = ATT_HEADS_PER_GROUP * ATT_DH
IN_SPLITS = (RET_QK_W, RET_QK_W, RET_V_W, RET_V_W, ATT_W, ATT_W, ATT_W, D_MODEL, D_MODEL)
IN_W = 9728


def _split_points(sizes):
    pts, acc = [], 0
    for s in sizes[:-1]:
        acc += s
        pts.append(acc)
    return pts

def rms_norm(x, g):
    xf = x.astype(jnp.float32)
    return xf * lax.rsqrt(jnp.mean(xf * xf, axis=-1, keepdims=True) + EPS) * g

def modulate(h, shift, scale):
    return h * (1.0 + scale[:, None, :]) + shift[:, None, :]

def rotary(t, pos):
    half = t.shape[-1] // 2
    inv = ROPE_BASE ** (-jnp.arange(half, dtype=jnp.float32) / half)
    ang = pos[:, None] * inv[None, :]
    cos, sin = jnp.cos(ang)[:, None, :], jnp.sin(ang)[:, None, :]
    t1, t2 = t[..., :half], t[..., half:]
    return jnp.concatenate([t1 * cos - t2 * sin, t1 * sin + t2 * cos], axis=-1)

def retention(q, k, v, g):
    B, S = q.shape[:2]
    H, dk, dv, C = RET_HEADS, RET_DK, RET_DV, RET_CHUNK
    nC = S // C
    pos = jnp.arange(S, dtype=jnp.float32)
    q = rotary(q.astype(jnp.float32).reshape(B, S, H, dk), pos)
    k = rotary(k.astype(jnp.float32).reshape(B, S, H, dk), pos) * (dk ** -0.5)
    v = v.astype(jnp.float32).reshape(B, S, H, dv)
    log_g = jnp.log1p(-jnp.exp2(-5.0 - jnp.arange(H, dtype=jnp.float32)))
    i = jnp.arange(C, dtype=jnp.float32)
    diff = i[:, None] - i[None, :]
    decay = jnp.where(diff[None] >= 0, jnp.exp(jnp.maximum(diff, 0.0)[None] * log_g[:, None, None]), 0.0)
    qc = q.reshape(B, nC, C, H, dk)
    kc = k.reshape(B, nC, C, H, dk)
    vc = v.reshape(B, nC, C, H, dv)
    scores = jnp.einsum('bnihd,bnjhd->bnhij', qc, kc) * decay
    inner = jnp.einsum('bnhij,bnjhe->bnihe', scores, vc)
    zeta = jnp.exp((C - 1.0 - i)[:, None] * log_g[None, :])
    kv = jnp.einsum('bnjhd,bnjhe->nbhde', kc * zeta[:, :, None], vc)
    g_chunk = jnp.exp(C * log_g)[None, :, None, None]

    def step(R, kv_n):
        return g_chunk * R + kv_n, R

    _, R_prev = lax.scan(step, jnp.zeros_like(kv[0]), kv)
    xi = jnp.exp((i + 1.0)[:, None] * log_g[None, :])
    cross = jnp.einsum('bnihd,nbhde->bnihe', qc * xi[:, :, None], R_prev)
    y = (inner + cross).reshape(B, S, H, dv)
    mu = jnp.mean(y, axis=-1, keepdims=True)
    var = jnp.mean(jnp.square(y - mu), axis=-1, keepdims=True)
    y = (y - mu) * lax.rsqrt(var + GN_EPS)
    return jax.nn.silu(g.astype(jnp.float32)) * y.reshape(B, S, H * dv)

def t5_bucket(dist):
    is_small = dist < REL_MAX_EXACT
    ratio = jnp.log(jnp.maximum(dist, 1).astype(jnp.float32) / REL_MAX_EXACT) / math.log(REL_MAX_DIST / REL_MAX_EXACT)
    large = REL_MAX_EXACT + (ratio * (REL_BUCKETS - REL_MAX_EXACT)).astype(jnp.int32)
    large = jnp.minimum(large, REL_BUCKETS - 1)
    return jnp.where(is_small, dist, large)

def dilated_attention(q, k, v, rel_bias):
    B, S = q.shape[:2]
    G, Hg, dh, QB = ATT_GROUPS, ATT_HEADS_PER_GROUP, ATT_DH, ATT_QBLOCK
    nb = S // QB
    q = q.reshape(B, S, G, Hg, dh)
    k = k.reshape(B, S, G, Hg, dh)
    v = v.reshape(B, S, G, Hg, dh)
    qb = q.reshape(B, nb, QB, G, Hg, dh).transpose(1, 0, 2, 3, 4, 5)
    ks = [k[:, :, g] for g in range(G)]
    vs = [v[:, :, g] for g in range(G)]
    biases = []
    for g, (w, r) in enumerate(ATT_PATTERNS):
        nk = w // r + 1
        bkt = t5_bucket(r * jnp.arange(nk, dtype=jnp.int32))
        biases.append(rel_bias[bkt, g * Hg:(g + 1) * Hg].T.astype(jnp.float32))
    scale = dh ** -0.5

    def block(args):
        n, qn = args
        pos = n * QB + jnp.arange(QB, dtype=jnp.int32)
        outs, lses = [], []
        for g, (w, r) in enumerate(ATT_PATTERNS):
            nk = w // r + 1
            idx = pos[:, None] - r * jnp.arange(nk, dtype=jnp.int32)[None, :]
            valid = idx >= 0
            idc = jnp.maximum(idx, 0)
            kg = jnp.take(ks[g], idc, axis=1)
            vg = jnp.take(vs[g], idc, axis=1)
            s = jnp.einsum('bqhd,bqjhd->bhqj', qn[:, :, g], kg).astype(jnp.float32) * scale
            s = s + biases[g][:, None, :]
            s = jnp.where(valid[None, None], s, -jnp.inf)
            m = jnp.max(s, axis=-1, keepdims=True)
            e = jnp.exp(s - m)
            l = jnp.sum(e, axis=-1, keepdims=True)
            o = jnp.einsum('bhqj,bqjhd->bqhd', e / l, vg.astype(jnp.float32))
            outs.append(o)
            lses.append((m + jnp.log(l))[..., 0].transpose(0, 2, 1))
        alpha = jax.nn.softmax(jnp.stack(lses, axis=0), axis=0)
        out = alpha[0][..., None] * outs[0]
        for g in range(1, G):
            out = out + alpha[g][..., None] * outs[g]
        return out

    out = lax.map(block, (jnp.arange(nb, dtype=jnp.int32), qb))
    return out.transpose(1, 0, 2, 3, 4).reshape(B, S, Hg * dh)

def moe(h, w_router, b_router, w1, b1, w2, b2):
    B, S, D = h.shape
    T = B * S
    xf = h.reshape(T, D)
    logits = (xf @ w_router + b_router).astype(jnp.float32)
    top_val, top_idx = lax.top_k(logits, TOP_K)
    gates = jax.nn.softmax(top_val, axis=-1)
    A = T * TOP_K
    flat_e = top_idx.reshape(A).astype(jnp.int32)
    flat_tok = jnp.arange(A, dtype=jnp.int32) // TOP_K
    flat_gate = gates.reshape(A)
    order = jnp.argsort(flat_e, stable=True)
    se = flat_e[order]
    counts = jnp.bincount(flat_e, length=N_EXPERTS)
    starts = jnp.cumsum(counts) - counts
    padded = (counts + MOE_BLOCK - 1) // MOE_BLOCK * MOE_BLOCK
    pend = jnp.cumsum(padded)
    pstart = pend - padded
    dest = pstart[se] + jnp.arange(A, dtype=jnp.int32) - starts[se]
    nblk = -(-A // MOE_BLOCK) + N_EXPERTS
    n_rows = nblk * MOE_BLOCK
    row_tok = jnp.full((n_rows,), T, jnp.int32).at[dest].set(flat_tok[order])
    row_gate = jnp.zeros((n_rows,), jnp.float32).at[dest].set(flat_gate[order])
    block_e = jnp.minimum(jnp.searchsorted(pend, jnp.arange(nblk, dtype=jnp.int32) * MOE_BLOCK, side='right'), N_EXPERTS - 1)
    x_pad = jnp.concatenate([xf, jnp.zeros((1, D), xf.dtype)], axis=0)
    xin = x_pad[row_tok].reshape(nblk, MOE_BLOCK, D)

    def expert_block(args):
        xb, e = args
        u = xb @ w1[e] + b1[e]
        glu = jnp.minimum(u[:, ::2], SWIGLU_LIMIT)
        lin = jnp.clip(u[:, 1::2], -SWIGLU_LIMIT, SWIGLU_LIMIT)
        a = glu * jax.nn.sigmoid(SWIGLU_ALPHA * glu) * (lin + 1.0)
        return a @ w2[e] + b2[e]

    yb = lax.map(expert_block, (xin, block_e)).reshape(n_rows, D)
    y = jnp.zeros((T + 1, D), jnp.float32).at[row_tok].add(yb.astype(jnp.float32) * row_gate[:, None])
    return y[:T].reshape(B, S, D)

def first_inputs(seed: int = 0) -> dict:
    key = jax.random.key(seed)
    ks = jax.random.split(key, 20)
    D, L, E, F = D_MODEL, DEPTH, N_EXPERTS, D_EXPERT
    nrm = jax.random.normal
    f32 = jnp.float32
    return {
        "x": nrm(ks[0], (BATCH, SEQ, D), f32),
        "c": nrm(ks[1], (BATCH, D), f32),
        "w_ada": nrm(ks[2], (L, D, 6 * D), f32) * (0.5 * D ** -0.5),
        "b_ada": nrm(ks[3], (L, 6 * D), f32) * 0.02,
        "g_mix": 1.0 + 0.02 * nrm(ks[4], (L, D), f32),
        "w_in": nrm(ks[5], (L, D, IN_W), f32) * D ** -0.5,
        "rel_bias": nrm(ks[6], (REL_BUCKETS, ATT_HEADS), f32) * 0.2,
        "w_ret_o": nrm(ks[7], (L, RET_V_W, D), f32) * RET_V_W ** -0.5,
        "w_att_o": nrm(ks[8], (L, ATT_OUT_W, D), f32) * ATT_OUT_W ** -0.5,
        "w_o": nrm(ks[9], (L, D, D), f32) * D ** -0.5,
        "g_ffn": 1.0 + 0.02 * nrm(ks[10], (L, D), f32),
        "w_router": nrm(ks[11], (L, D, E), f32) * D ** -0.5,
        "b_router": nrm(ks[12], (L, E), f32) * 0.01,
        "w_mlp1": nrm(ks[13], (L, E, D, 2 * F), f32) * D ** -0.5,
        "b_mlp1": nrm(ks[14], (L, E, 2 * F), f32) * 0.01,
        "w_mlp2": nrm(ks[15], (L, E, F, D), f32) * F ** -0.5,
        "b_mlp2": nrm(ks[16], (L, E, D), f32) * 0.01,
        "g_final": 1.0 + 0.02 * nrm(ks[17], (D,), f32),
    }

def first_block(x, c, w_ada, b_ada, g_mix, w_in, rel_bias, w_ret_o, w_att_o, w_o, g_ffn,
              w_router, b_router, w_mlp1, b_mlp1, w_mlp2, b_mlp2, g_final):
    cs = jax.nn.silu(c.astype(jnp.float32))
    pts = _split_points(IN_SPLITS)
    for l in range(DEPTH):
        mod = cs @ w_ada[l] + b_ada[l]
        sh_a, sc_a, gt_a, sh_f, sc_f, gt_f = jnp.split(mod, 6, axis=-1)
        h = modulate(rms_norm(x, g_mix[l]), sh_a, sc_a)
        u = h @ w_in[l]
        rq, rk, rv, rg, aq, ak, av, ga, gb = jnp.split(u, pts, axis=-1)
        ret = retention(rq, rk, rv, rg)
        att = dilated_attention(aq, ak, av, rel_bias)
        merged = jax.nn.sigmoid(ga) * (ret @ w_ret_o[l]) + jax.nn.sigmoid(gb) * (att @ w_att_o[l])
        x = x + gt_a[:, None, :] * (merged @ w_o[l])
        h = modulate(rms_norm(x, g_ffn[l]), sh_f, sc_f)
        x = x + gt_f[:, None, :] * moe(h, w_router[l], b_router[l], w_mlp1[l], b_mlp1[l], w_mlp2[l], b_mlp2[l])
    return rms_norm(x, g_final)


DEPTH_2 = 2

N_MIXERS = 2
HEAD_DIM = 64
N_MIX_HEADS = 12
W_MIX = N_MIX_HEADS * HEAD_DIM
N_MEM_HEADS = 4
W_MEM = N_MEM_HEADS * HEAD_DIM
N_MEM = 256
GMLP_CHUNK = 128
MOBA_BLOCK = 256
MOBA_TOPK = 3
MOBA_Q_BLOCK = 64
D_FF = int(math.ceil(8 * D_MODEL / 3 / 256) * 256)
ALPHA = (2.0 * DEPTH_2) ** 0.25
BETA = (8.0 * DEPTH_2) ** -0.25
LN_EPS = 1e-5


def layer_norm(x, g, b):
    xf = x.astype(jnp.float32)
    mu = jnp.mean(xf, axis=-1, keepdims=True)
    var = jnp.mean(jnp.square(xf - mu), axis=-1, keepdims=True)
    y = (xf - mu) * lax.rsqrt(var + LN_EPS)
    return (y * g.astype(jnp.float32) + b.astype(jnp.float32)).astype(x.dtype)

def gmlp_mixer(u, v, ln_g, ln_b, w_s, b_s):
    B, S, _ = u.shape
    u = jax.nn.gelu(u)
    v = layer_norm(jax.nn.gelu(v), ln_g, ln_b)
    vc = v.reshape(B, S // GMLP_CHUNK, GMLP_CHUNK, N_MIX_HEADS, HEAD_DIM)
    causal = jnp.tril(jnp.ones((GMLP_CHUNK, GMLP_CHUNK), w_s.dtype))
    w = w_s * causal[None]
    sv = jnp.einsum('gts,bcsgd->bctgd', w, vc) + b_s.T[None, None, :, :, None]
    return u * sv.reshape(B, S, W_MIX)

def moba_attention(q, k, v):
    B, S, H, dh = q.shape
    n_blk = -(-S // MOBA_BLOCK)
    Sp = n_blk * MOBA_BLOCK
    pad = ((0, 0), (0, Sp - S), (0, 0), (0, 0))
    qh = jnp.pad(q, pad).transpose(0, 2, 1, 3)
    kb = jnp.pad(k, pad).transpose(0, 2, 1, 3).reshape(B, H, n_blk, MOBA_BLOCK, dh)
    vb = jnp.pad(v, pad).transpose(0, 2, 1, 3).reshape(B, H, n_blk, MOBA_BLOCK, dh)
    k_mean = jnp.mean(kb.astype(jnp.float32), axis=3)
    topk = min(MOBA_TOPK, n_blk)
    scale = dh ** -0.5
    b_idx = jnp.arange(B)[:, None, None, None]
    h_idx = jnp.arange(H)[None, :, None, None]

    def one_query_block(c):
        start = c * MOBA_Q_BLOCK
        qc = lax.dynamic_slice_in_dim(qh, start, MOBA_Q_BLOCK, axis=2)
        j = start // MOBA_BLOCK
        blk_s = jnp.einsum('bhqd,bhnd->bhqn', qc.astype(jnp.float32), k_mean)
        blk_s = jnp.where(jnp.arange(n_blk) < j, blk_s, -jnp.inf)
        _, sel = lax.top_k(blk_s, topk)
        valid = jnp.arange(topk) < j
        k_sel = kb[b_idx, h_idx, sel]
        v_sel = vb[b_idx, h_idx, sel]
        s_sel = jnp.einsum('bhqd,bhqnkd->bhqnk', qc, k_sel).astype(jnp.float32) * scale
        s_sel = jnp.where(valid[:, None], s_sel, -jnp.inf)
        k_own = lax.dynamic_index_in_dim(kb, j, axis=2, keepdims=False)
        v_own = lax.dynamic_index_in_dim(vb, j, axis=2, keepdims=False)
        s_own = jnp.einsum('bhqd,bhkd->bhqk', qc, k_own).astype(jnp.float32) * scale
        q_pos = start + jnp.arange(MOBA_Q_BLOCK)
        k_pos = j * MOBA_BLOCK + jnp.arange(MOBA_BLOCK)
        s_own = jnp.where(k_pos[None, :] <= q_pos[:, None], s_own, -jnp.inf)
        s_all = jnp.concatenate(
            [s_sel.reshape(B, H, MOBA_Q_BLOCK, topk * MOBA_BLOCK), s_own], axis=-1)
        p = jax.nn.softmax(s_all, axis=-1)
        p_sel = p[..., :topk * MOBA_BLOCK].reshape(B, H, MOBA_Q_BLOCK, topk, MOBA_BLOCK)
        p_own = p[..., topk * MOBA_BLOCK:]
        out = (jnp.einsum('bhqnk,bhqnkd->bhqd', p_sel.astype(v.dtype), v_sel)
               + jnp.einsum('bhqk,bhkd->bhqd', p_own.astype(v.dtype), v_own))
        return out

    outs = lax.map(one_query_block, jnp.arange(Sp // MOBA_Q_BLOCK))
    out = outs.transpose(1, 2, 0, 3, 4).reshape(B, H, Sp, dh)
    return out.transpose(0, 2, 1, 3)[:, :S]

def memory_cross_attention(q_mem, mem, w_kv):
    B, S, _ = q_mem.shape
    q = q_mem.reshape(B, S, N_MEM_HEADS, HEAD_DIM)
    kv = mem @ w_kv
    k, v = jnp.split(kv, 2, axis=-1)
    k = k.reshape(B, -1, N_MEM_HEADS, HEAD_DIM)
    v = v.reshape(B, -1, N_MEM_HEADS, HEAD_DIM)
    s = jnp.einsum('bshd,bmhd->bhsm', q, k).astype(jnp.float32) * HEAD_DIM ** -0.5
    p = jax.nn.softmax(s, axis=-1).astype(v.dtype)
    return jnp.einsum('bhsm,bmhd->bshd', p, v).reshape(B, S, W_MEM)

def swiglu(x, w_in, w_out):
    g, u = jnp.split(x @ w_in, 2, axis=-1)
    return (jax.nn.silu(g) * u) @ w_out

def second_inputs(seed: int = 0) -> dict:
    key = jax.random.key(seed)
    ks = jax.random.split(key, 16)
    n_a = (DEPTH_2 + 1) // 2
    n_b = DEPTH_2 // 2
    D = D_MODEL
    nrm = jax.random.normal
    f32 = jnp.float32
    return {
        "x": nrm(ks[0], (BATCH, SEQ, D), f32),
        "mem": nrm(ks[1], (BATCH, N_MEM, D), f32),
        "a_w_in": nrm(ks[2], (n_a, D, 2 * W_MIX + W_MEM), f32) * D ** -0.5,
        "a_ln_v_g": 1.0 + 0.02 * nrm(ks[3], (n_a, W_MIX), f32),
        "a_ln_v_b": 0.02 * nrm(ks[4], (n_a, W_MIX), f32),
        "a_w_s": nrm(ks[5], (n_a, N_MIX_HEADS, GMLP_CHUNK, GMLP_CHUNK), f32) * GMLP_CHUNK ** -0.5,
        "a_b_s": 1.0 + 0.1 * nrm(ks[6], (n_a, N_MIX_HEADS, GMLP_CHUNK), f32),
        "b_w_in": nrm(ks[7], (n_b, D, 3 * W_MIX + W_MEM), f32) * D ** -0.5,
        "w_mem_kv": nrm(ks[8], (DEPTH_2, D, 2 * W_MEM), f32) * D ** -0.5,
        "w_mix_out": nrm(ks[9], (DEPTH_2, W_MIX + W_MEM, D), f32) * (W_MIX + W_MEM) ** -0.5 * BETA,
        "ln_mix_g": 1.0 + 0.02 * nrm(ks[10], (DEPTH_2, D), f32),
        "ln_mix_b": 0.02 * nrm(ks[11], (DEPTH_2, D), f32),
        "w_ffn_in": nrm(ks[12], (DEPTH_2, D, 2 * D_FF), f32) * D ** -0.5,
        "w_ffn_out": nrm(ks[13], (DEPTH_2, D_FF, D), f32) * D_FF ** -0.5 * BETA,
        "ln_ffn_g": 1.0 + 0.02 * nrm(ks[14], (DEPTH_2, D), f32),
        "ln_ffn_b": 0.02 * nrm(ks[15], (DEPTH_2, D), f32),
    }

def second_block(x, mem, a_w_in, a_ln_v_g, a_ln_v_b, a_w_s, a_b_s, b_w_in, w_mem_kv,
              w_mix_out, ln_mix_g, ln_mix_b, w_ffn_in, w_ffn_out, ln_ffn_g, ln_ffn_b):
    B, S, _ = x.shape
    for i in range(DEPTH_2):
        li = i // N_MIXERS
        if i % N_MIXERS == 0:
            h = x @ a_w_in[li]
            u, v, q_mem = jnp.split(h, [W_MIX, 2 * W_MIX], axis=-1)
            mix = gmlp_mixer(u, v, a_ln_v_g[li], a_ln_v_b[li], a_w_s[li], a_b_s[li])
        else:
            h = x @ b_w_in[li]
            q, k, v, q_mem = jnp.split(h, [W_MIX, 2 * W_MIX, 3 * W_MIX], axis=-1)
            shp = (B, S, N_MIX_HEADS, HEAD_DIM)
            mix = moba_attention(q.reshape(shp), k.reshape(shp), v.reshape(shp)).reshape(B, S, W_MIX)
        mem_out = memory_cross_attention(q_mem, mem, w_mem_kv[i])
        sub = jnp.concatenate([mix, mem_out], axis=-1) @ w_mix_out[i]
        x = layer_norm(ALPHA * x + sub, ln_mix_g[i], ln_mix_b[i])
        x = layer_norm(ALPHA * x + swiglu(x, w_ffn_in[i], w_ffn_out[i]), ln_ffn_g[i], ln_ffn_b[i])
    return x


def setup_inputs(seed=0):
    out = dict(first_inputs(seed))
    for name, value in second_inputs(seed + 1).items():
        if name != "x":
            out[name + "_2"] = value
    return out


def reference(
    x, c, w_ada, b_ada, g_mix, w_in, rel_bias, w_ret_o, w_att_o, w_o, g_ffn, w_router, b_router,
    w_mlp1, b_mlp1, w_mlp2, b_mlp2, g_final, mem_2, a_w_in_2, a_ln_v_g_2, a_ln_v_b_2, a_w_s_2,
    a_b_s_2, b_w_in_2, w_mem_kv_2, w_mix_out_2, ln_mix_g_2, ln_mix_b_2, w_ffn_in_2, w_ffn_out_2,
    ln_ffn_g_2, ln_ffn_b_2,
):
    x = first_block(
        x, c, w_ada, b_ada, g_mix, w_in, rel_bias, w_ret_o, w_att_o, w_o, g_ffn, w_router,
        b_router, w_mlp1, b_mlp1, w_mlp2, b_mlp2, g_final,
    )
    return second_block(
        x, mem_2, a_w_in_2, a_ln_v_g_2, a_ln_v_b_2, a_w_s_2, a_b_s_2, b_w_in_2, w_mem_kv_2,
        w_mix_out_2, ln_mix_g_2, ln_mix_b_2, w_ffn_in_2, w_ffn_out_2, ln_ffn_g_2, ln_ffn_b_2,
    )


_drawn_inputs = setup_inputs


def setup_inputs(seed=0):
    import zlib

    import numpy as np

    out = dict(_drawn_inputs(seed))
    spreads = {}
    factors = {'g_mix': 4.208,
     'rel_bias': 5.609,
     'g_ffn': 3.565,
     'b_router': 5.51,
     'b_mlp1': 8.0,
     'b_mlp2': 45.157,
     'g_final': 2.715,
     'a_ln_v_g_2': 89.906,
     'a_ln_v_b_2': 91.574,
     'a_b_s_2': 8.948,
     'mem_2': 2.758,
     'w_mem_kv_2': 2.694}
    for name, (base, spread) in spreads.items():
        noise = np.random.default_rng([zlib.crc32(name.encode()), seed]).standard_normal(out[name].shape)
        drawn = base * np.exp(spread * noise) if base else spread * noise
        out[name] = __import__('jax').numpy.asarray(drawn.astype(out[name].dtype))
    for name, factor in factors.items():
        out[name] = (out[name] * factor).astype(out[name].dtype)
    return out
```

```python
import math
from contextlib import ExitStack

import numpy as np

import concourse.bass as bass
from concourse import mybir

FP32 = mybir.dt.float32
I32 = mybir.dt.int32
ALU = mybir.AluOpType
ACT = mybir.ActivationFunctionType
AX = mybir.AxisListType

P = 128
S = 256
T = S // P
D = 1024
KC = D // P
N = 512
IN_W = 9728
RH, RDK, RDV = 4, 128, 256
PATTERNS = ((128, 1), (512, 4), (2048, 16))
AG, AH, ADH = 3, 4, 128
BUCKETS, MAX_EXACT, MAX_DIST = 32, 16, 2048
E = 32
CAP = 64
ROUNDS = S // CAP
LIMIT, SWISH = 7.0, 1.702
EPS, GN_EPS, LN_EPS = 1e-6, 1e-5, 1e-5
NEG = -1.0e30
HEADS, DH = 12, 64
W_MIX, W_MEM, M_HEADS, N_MEM = HEADS * DH, 256, 4, 256
F2 = int(math.ceil(8 * D / 3 / 256) * 256)
FC2 = F2 // P
ALPHA = 4.0 ** 0.25
SLOT = 2048
RING = 12
BANKS = 8
TAB = 384
ARENA = 20480

_COLS = (("ident", P), ("anti", P), ("before", P), ("upto", P), ("ones", P), ("causal", S),
         ("cos", T * 64), ("sin", T * 64), ("decay", 2 * RH * P), ("slots", ROUNDS * P))
AT, _at = {}, 0
for _name, _width in _COLS:
    AT[_name] = (_at, _width)
    _at += _width
CONST_W = _at


def bucket_of(dist):
    ratio = np.log(np.maximum(dist, 1).astype(np.float32) / np.float32(MAX_EXACT)) / np.float32(math.log(MAX_DIST / MAX_EXACT))
    large = np.minimum(MAX_EXACT + (ratio * np.float32(BUCKETS - MAX_EXACT)).astype(np.int32), BUCKETS - 1)
    return np.where(dist < MAX_EXACT, dist, large)


def shape_constants():
    table = np.zeros((P, CONST_W), np.float32)

    def put(name, value):
        a, w = AT[name]
        table[:, a:a + w] = np.asarray(value, np.float32).reshape(P, w)

    i = np.arange(P)
    put("ident", np.eye(P))
    put("anti", np.eye(P)[::-1])
    put("before", i[:, None] < i[None, :])
    put("upto", i[:, None] <= i[None, :])
    put("ones", np.ones((P, P)))
    q, k = np.arange(P)[:, None] + P, np.arange(S)[None, :]
    put("causal", np.where(k <= q, 0.0, NEG))
    half = RDK // 2
    inv = np.float32(10000.0) ** (-np.arange(half, dtype=np.float32) / np.float32(half))
    pos = np.arange(S, dtype=np.float32).reshape(T, P).T
    ang = (pos[:, :, None] * inv[None, None, :]).astype(np.float32)
    put("cos", np.cos(ang))
    put("sin", np.sin(ang))
    log_g = np.log1p(-np.exp2(-5.0 - np.arange(RH)))
    diff = i[None, :] - i[:, None] + P * np.arange(2)[:, None, None]
    decay = np.where(diff[:, None] >= 0, np.exp(np.maximum(diff, 0)[:, None] * log_g[None, :, None, None]), 0.0)
    put("decay", decay.transpose(2, 0, 1, 3) * RDK ** -0.5)
    put("slots", np.broadcast_to(CAP * np.arange(ROUNDS)[:, None, None] + np.arange(CAP)[None, None, :], (P, ROUNDS, 2, CAP)))
    onehot = np.zeros((BUCKETS + 1, AG, TAB), np.float32)
    dist = S - 1 - np.arange(TAB)
    for g, (w, r) in enumerate(PATTERNS):
        ok = (dist >= 0) & (dist % r == 0) & (dist // r <= w // r)
        onehot[bucket_of(np.maximum(dist, 0)), g, np.arange(TAB)] = ok
        onehot[BUCKETS, g] = np.where(ok, 0.0, NEG)
    return table, onehot


class Job:
    def __init__(self, index, name, by, slots):
        self.index, self.name, self.by, self.slots = index, name, by, slots
        self.freed = None


class Jobs:

    def __init__(self, banks, slots):
        self.banks, self.slots, self.list, self.by_name, self.last_use = banks, slots, [], {}, {}
        self.counts = {"act": 0, "dve": 0}

    def add(self, name, by, slots=()):
        job = Job(len(self.list), name, by, list(slots))
        self.counts[by] += 1
        job.freed = self.counts[by]
        self.list.append(job)
        self.by_name[name] = job
        for q in slots:
            self.last_use[q] = job.index
        return job

    def full(self, name):
        return self.by_name[name].index + 1

    def bank(self, name):
        return self.by_name[name].index % self.banks


class Chain:

    def __init__(self, eng, sem):
        self.eng, self.sem, self.n = eng, sem, 0

    def __call__(self, ins):
        self.n += 1
        ins.then_inc(self.sem, 1)
        self.eng.wait_ge(self.sem, self.n)

    def mark(self, ins):
        self.n += 1
        ins.then_inc(self.sem, 1)

    def sync(self):
        self.eng.wait_ge(self.sem, self.n)


def free(tile, at, *shape):
    w = int(np.prod(shape))
    v = tile[:, at:at + w]
    if len(shape) == 1:
        return v
    names = "abcd"[:len(shape)]
    return v.rearrange("p (%s) -> p %s" % (" ".join(names), " ".join(names)), **{n: s for n, s in zip(names[1:], shape[1:])})


def const(M, name, *shape):
    a, w = AT[name]
    return free(M["const"], a, *(shape or (w,)))


def k_slots(w, col, width=N):
    half = KC // 2
    return [w[half * P * i:half * P * (i + 1), col:col + width].rearrange("(k p) n -> p k n", p=P) for i in range(w.shape[0] // (half * P))]


def mixer(nc, M, A, scratch):
    x_sb, actT, ring, arena, bank = M["x"], M["actT"], M["ring"], M["arena"], M["bank"]
    slots_in_ring = RING - 2
    spare = ring[:, slots_in_ring * SLOT:RING * SLOT]

    rot = free(arena, 0, T, 2, RH, RDK)
    hnat = free(arena, 0, T, D)
    ynat = free(arena, 0, T, D)
    sga = free(arena, 0, T, D)
    qkT = free(arena, 2048, 2, RH, S)
    retT = free(arena, 2048, KC, S)
    rv = free(arena, 4096, T, D)
    sgb = free(arena, 4096, T, D)
    rg = free(arena, 6144, T, D)
    attT = free(arena, 6144, AH, S)
    aqT = free(arena, 8192, AG * AH, S)
    akT = free(arena, 11264, AG * AH, S)
    rows_mod = free(arena, 8192, 4, D)
    gs, sh, g_row = free(arena, 14336, D), free(arena, 15360, D), free(arena, 16384, D)
    av = free(arena, 14336, T, AG * AH * ADH)
    g_ffn_row = free(arena, 12288, D)
    probs = free(arena, 17408, 2, AG, S)
    sT = free(arena, 17408, 2, 2, P)
    rtmp = free(arena, 18432, 2, RH, 64)
    onehot = arena[0:BUCKETS + 1, 17408:17408 + AG * TAB].rearrange("p (g n) -> p g n", g=AG)
    probsT = free(arena, 18944, 2, 2 * AG, P)
    tab = arena[0:AH, 18944:18944 + AG * TAB].rearrange("p (g n) -> p g n", g=AG)
    hankel = free(spare, 0, AG, AH, S)
    mod4 = free(spare, 3072, N)
    small = M["small"]
    sumsq, rstd = small[:, 0:2], small[:, 2:4]
    cs, bias_rel = small[:, 8:16], small[0:BUCKETS + 1, 16:28]
    stats, mv = free(small, 32, RH, 6), free(small, 64, RH, 2)
    rstd4 = small[:, 72:76]
    negmax, mx2, lsum, rsum = small[:, 80:82], free(small, 84, 2, 2), free(small, 88, 2, 2), small[:, 92:94]
    csb = free(small, 128, KC, 32)
    c8, b12 = M["c8"], M["b12"]
    ident = const(M, "ident")

    slots = []

    def rows_of_ada(g):
        first = len(slots)
        for k in range(KC):
            slots.append(A["w_ada"][0, k * P:(k + 1) * P, SLOT * g:SLOT * (g + 1)].rearrange("p (k n) -> p k n", k=4))
        return list(range(first, len(slots)))

    def chunk(w, col):
        new = k_slots(w, col)
        slots.extend(new)
        return list(range(len(slots) - len(new), len(slots)))

    jobs = Jobs(BANKS, slots)

    jobs.add("cT", "act")
    for g in range(AG):
        jobs.add(f"tab{g}", "act")
    jobs.add("ada0", "dve", rows_of_ada(0))
    for n in range(4):
        jobs.add(f"mod{n}", "act" if n < 2 else "dve")
    for t in range(T):
        for half in range(2):
            jobs.add(f"hT{t}{half}", "act" if half else "dve")
    w_in = A["w_in"][0]
    for name, col in (("rq", 0), ("rk", 512), ("rv0", 1024), ("rv1", 1536)):
        c = chunk(w_in, col)
        for t in range(T):
            jobs.add(f"{name}t{t}", "dve" if name in ("rq", "rk") else "act", c)
    for i in range(2):
        for t in range(T):
            jobs.add(f"rT{i}{t}", "act")
    for i in range(2):
        c = chunk(w_in, 2048 + N * i)
        for t in range(T):
            jobs.add(f"rg{i}t{t}", "act", c)
    units = [(h, t) for h in range(RH) for t in range(T)]
    fill = []
    for u in range(len(units) + 1):
        fill.append(([(f"rs{u}", "dve")] if u < len(units) else []) + ([(f"ry{u - 1}", "dve")] if u else []))
    fill += [[], [], [(f"retT{n}", "act") for n in range(4)]]
    for what, col in (("aq", 3072), ("ak", 4608)):
        for g in range(AG):
            c = chunk(w_in, col + N * g)
            for h in range(AH):
                jobs.add(f"{what}{AH * g + h}", "act", c)
                for name, by in (fill.pop(0) if fill else []):
                    jobs.add(name, by)
    for g in range(AG):
        c = chunk(w_in, 6144 + N * g)
        for t in range(T):
            jobs.add(f"av{g}t{t}", "act", c)
    filler = []
    for what, w, col, by in (("ga", w_in, 7680, "act"), ("gb", w_in, 8704, "act"), ("ro", A["w_ret_o"][0], 0, "dve")):
        for half in range(2):
            c = chunk(w, col + N * half)
            for t in range(T):
                filler.append((f"{what}{half}t{t}", by, c))
    for u in range(len(units) + 1):
        if u < len(units):
            jobs.add(f"sa{u}", "act")
            jobs.add(f"sb{u}", "act")
        if filler:
            jobs.add(*filler.pop(0))
        if u:
            for n in range(1 + units[u - 1][1]):
                jobs.add(f"pT{u - 1}{n}", "act")
            if filler:
                jobs.add(*filler.pop(0))
            jobs.add(f"ao{u - 1}", "dve")
    assert not filler
    for half in range(2):
        c = chunk(A["w_att_o"][0], N * half)
        for t in range(T):
            jobs.add(f"to{half}t{t}", "dve", c)
    for g in (1, 2):
        jobs.add(f"ada{g}", "dve", rows_of_ada(g))
        for n in range(4 * g, 4 * g + 4):
            jobs.add(f"mod{n}", "dve" if n in (8, 9) else "act")
    for t in range(T):
        for half in range(2):
            jobs.add(f"mT{t}{half}", "act" if half else "dve")
    for half in range(2):
        c = chunk(A["w_o"][0], N * half)
        for t in range(T):
            jobs.add(f"wo{half}t{t}", "dve", c)

    ctx = ExitStack()
    with ctx:
        def sem(name):
            return ctx.enter_context(nc.semaphore("mix_" + name))

        full, freed_by_act, freed_by_dve = sem("full"), sem("freed_by_act"), sem("freed_by_dve")
        freed = {"act": freed_by_act, "dve": freed_by_dve}
        slot_here = [sem(f"slot_here{i}") for i in range(slots_in_ring)]
        const_here, x_here, row_here, tiny_here, rel_here = sem("const_here"), sem("x_here"), sem("row_here"), sem("tiny_here"), sem("rel_here")
        ffn_row_here = sem("ffn_row_here")
        rel_ready, table_out, bias_here = sem("rel_ready"), sem("table_out"), sem("bias_here")
        dve_step, act_step = sem("dve_step"), sem("act_step")
        squares_ready, mean_ready, root_ready = sem("squares_ready"), sem("mean_ready"), sem("root_ready")
        cs_ready, csb_ready, h_ready, rot_ready = sem("cs_ready"), sem("csb_ready"), sem("h_ready"), sem("rot_ready")
        var_ready, ret_root_ready, ret_ready = sem("var_ready"), sem("ret_root_ready"), sem("ret_ready")
        max_ready, probs_ready, merged_ready, x_ready = sem("max_ready"), sem("probs_ready"), sem("merged_ready"), sem("x_ready")
        block = ctx.enter_context(nc.Block())

        def wait_freed(eng, name):
            job = jobs.by_name[name]
            eng.wait_ge(freed[job.by], job.freed)

        @block.sync
        def _(sp):
            sp.dma_start(M["c8"][:, :], A["c"][0].rearrange("(k p) -> k p", p=P)).then_inc(tiny_here, 16)
            sp.dma_start(M["b12"][:, :], A["b_ada"][0].rearrange("(k n) -> k n", n=N)).then_inc(tiny_here, 16)
            sp.dma_start(M["const"][:, :], A["table"]).then_inc(const_here, 16)
            sp.dma_start(x_sb[:, :, :], A["x"][0].rearrange("(t p) d -> p t d", p=P)).then_inc(x_here, 16)
            sp.dma_start(g_row.unsqueeze(1), A["g_mix"][0:1, :].partition_broadcast(P)).then_inc(row_here, 16)
            for q, src in enumerate(slots):
                s = q % slots_in_ring
                if q >= slots_in_ring:
                    sp.wait_ge(full, jobs.last_use[q - slots_in_ring] + 1)
                dst = ring[:, s * SLOT:(s + 1) * SLOT].rearrange("p (k n) -> p k n", n=src.shape[2])
                sp.dma_start(dst, src).then_inc(slot_here[s], 16)
            sp.wait_ge(full, jobs.full("ada1"))

        @block.gpsimd
        def _(pool):
            pool.memset(bias_rel[BUCKETS:BUCKETS + 1, :], 1.0).then_inc(rel_ready, 1)
            pool.dma_start(bias_rel[0:BUCKETS, :], A["rel_bias"]).then_inc(rel_here, 16)
            pool.dma_start(onehot, A["onehot"]).then_inc(rel_here, 16)
            wait_freed(pool, "tab2")
            pool.dma_start(scratch.rearrange("(g h) n -> h g n", g=AG), tab).then_inc(table_out, 16)
            pool.wait_ge(table_out, 16)
            for g in range(AG):
                shifted = bass.AP(tensor=scratch.tensor, offset=g * AH * TAB, ap=[[1, P], [TAB, AH], [1, S]])
                pool.dma_start(hankel[:, g], shifted).then_inc(bias_here, 16)
            pool.wait_ge(full, jobs.full("sb7"))
            pool.dma_start(g_ffn_row.unsqueeze(1), A["g_ffn"][0:1, :].partition_broadcast(P)).then_inc(ffn_row_here, 16)
            pool.wait_ge(ffn_row_here, 16)

        @block.scalar
        def _(act):
            chain = Chain(act, act_step)

            def rms_roots(src):
                for t in range(T):
                    nc.scalar.activation(hnat[:, t, :], src[:, t, :], ACT.Square, accum_out=sumsq[:, t:t + 1]).then_inc(squares_ready, 1)
                act.wait_ge(mean_ready, 1)
                nc.scalar.activation(rstd, rstd, ACT.Sqrt).then_inc(root_ready, 1)

            act.wait_ge(x_here, 16)
            rms_roots(x_sb)
            for job in jobs.list:
                name, b = job.name, bank[job.index % BANKS]
                if job.by != "act":
                    if name == "ry7":
                        act.wait_ge(var_ready, 1)
                        nc.scalar.activation(M["var8"], M["var8"], ACT.Sqrt).then_inc(ret_root_ready, 1)
                    continue
                act.wait_ge(full, job.index + 1)
                last = None
                if name == "cT":
                    last = nc.scalar.activation(cs, b[:, 0:KC], ACT.Silu)
                elif name.startswith("tab"):
                    last = nc.scalar.copy(tab[:, int(name[3:]), :], b[0:AH, 0:TAB])
                elif name.startswith("mod"):
                    n = int(name[3:])
                    if n < 4:
                        dst = sh[:, N * n:N * n + N]
                    else:
                        dst = rows_mod[:, {4: 0, 6: 1, 10: 3}[n - n % 2], N * (n % 2):N * (n % 2) + N]
                    last = nc.scalar.copy(dst, b)
                elif name.startswith("hT") or name.startswith("mT"):
                    t, half = int(name[2]), int(name[3])
                    last = nc.scalar.copy(actT[:, 4 * half:4 * half + 4, P * t:P * t + P], b.rearrange("p (k s) -> p k s", k=4))
                elif name.startswith("rv"):
                    i, t = int(name[2]), int(name[4])
                    last = nc.scalar.copy(rv[:, t, N * i:N * i + N], b)
                elif name.startswith("rT"):
                    i, t = int(name[2]), int(name[3])
                    last = nc.scalar.copy(qkT[:, i, :, P * t:P * t + P], b.rearrange("p (h s) -> p h s", h=RH))
                elif name.startswith("rg"):
                    i, t = int(name[2]), int(name[4])
                    last = nc.scalar.activation(rg[:, t, N * i:N * i + N], b, ACT.Silu)
                elif name.startswith("retT"):
                    n = int(name[4])
                    last = nc.scalar.copy(retT[:, 4 * (n % 2):4 * (n % 2) + 4, P * (n // 2):P * (n // 2) + P], b.rearrange("p (k s) -> p k s", k=4))
                elif name.startswith("aq"):
                    last = nc.scalar.mul(aqT[:, int(name[2:]), :], b[:, 0:S], ADH ** -0.5)
                elif name.startswith("ak"):
                    last = nc.scalar.copy(akT[:, int(name[2:]), :], b[:, 0:S])
                elif name.startswith("av"):
                    g, t = int(name[2]), int(name[4])
                    last = nc.scalar.copy(av[:, t, N * g:N * g + N], b)
                elif name.startswith("ga") or name.startswith("gb"):
                    half, t = int(name[2]), int(name[4])
                    dst = sga if name[1] == "a" else sgb
                    last = nc.scalar.activation(dst[:, t, N * half:N * half + N], b, ACT.Sigmoid)
                elif name[:2] in ("sa", "sb"):
                    u = int(name[2:])
                    h, t = units[u]
                    w, part = P * (t + 1), "ab".index(name[1])
                    act.wait_ge(max_ready, u + 1)
                    groups = 1 if part else 2
                    src = b.rearrange("p (g k) -> p g k", k=S)[:, 0:groups, 0:w]
                    last = nc.scalar.activation(probs[:, u % 2, 2 * part:2 * part + groups, 0:w], src, ACT.Exp,
                                                bias=negmax[:, u % 2:u % 2 + 1], accum_out=lsum[:, u % 2, part:part + 1])
                elif name.startswith("pT"):
                    u, n = int(name[2:-1]), int(name[-1])
                    last = nc.scalar.copy(probsT[:, u % 2, AG * n:AG * n + AG, :], b[:, 0:AG * P].rearrange("p (g s) -> p g s", g=AG))
                last.then_inc(freed_by_act, 1)

        @block.vector
        def _(dve):
            step = Chain(dve, dve_step)
            dve.wait_ge(squares_ready, T)
            nc.vector.tensor_scalar(rstd, sumsq, 1.0 / D, EPS, ALU.mult, ALU.add).then_inc(mean_ready, 1)
            dve.wait_ge(root_ready, 1)
            step(nc.vector.reciprocal(rstd, rstd))
            wait_freed(dve, "cT")
            nc.vector.tensor_copy(csb, cs.unsqueeze(2).to_broadcast([P, KC, 32])).then_inc(csb_ready, 1)
            dve.wait_ge(x_here, 16)
            for t in range(T):
                step.mark(nc.vector.tensor_scalar(hnat[:, t, :], x_sb[:, t, :], rstd[:, t:t + 1], None, ALU.mult))
            step.sync()
            dve.wait_ge(const_here, 16)
            cos, sin = const(M, "cos", T, 64), const(M, "sin", T, 64)
            decay = const(M, "decay", 2, RH, P)
            for job in jobs.list:
                name, b = job.name, bank[job.index % BANKS]
                if job.by != "dve":
                    if name[:2] == "sb":
                        u = int(name[2:])
                        w = P * (units[u][1] + 1)
                        ba = bank[jobs.bank(f"sa{u}")].rearrange("p (g k) -> p g k", k=S)[:, :, 0:w]
                        dve.wait_ge(full, jobs.full(name))
                        step.mark(nc.vector.tensor_reduce(mx2[:, u % 2, 0:1], ba, AX.XY, ALU.max))
                        step(nc.vector.tensor_reduce(mx2[:, u % 2, 1:2], b[:, 0:w], AX.X, ALU.max))
                        nc.vector.tensor_reduce(negmax[:, u % 2:u % 2 + 1], mx2[:, u % 2, :], AX.X, ALU.max, negate=True).then_inc(max_ready, 1)
                    if name[:2] == "pT" and name[-1] == "0":
                        u = int(name[2:-1])
                        w = P * (units[u][1] + 1)
                        wait_freed(dve, f"sb{u}")
                        step(nc.vector.tensor_tensor(rsum[:, u % 2:u % 2 + 1], lsum[:, u % 2, 0:1], lsum[:, u % 2, 1:2], ALU.add))
                        step(nc.vector.reciprocal(rsum[:, u % 2:u % 2 + 1], rsum[:, u % 2:u % 2 + 1]))
                        pr = probs[:, u % 2, :, 0:w]
                        nc.vector.tensor_scalar(pr, pr, rsum[:, u % 2:u % 2 + 1], None, ALU.mult).then_inc(probs_ready, 1)
                    continue
                if name.startswith("ada"):
                    dve.wait_ge(full, job.index + 1)
                    nc.vector.tensor_copy(mod4, b).then_inc(freed_by_dve, 1)
                    continue
                if name.startswith("mod"):
                    n = int(name[3:])
                    dve.wait_ge(full, job.index + 1)
                    half = N * (n % 2)
                    if n < 4:
                        dve.wait_ge(row_here, 16)
                        dst, row = gs, g_row
                    else:
                        dve.wait_ge(ffn_row_here, 16)
                        dst, row = rows_mod[:, 2, :], g_ffn_row
                    nc.vector.scalar_tensor_tensor(dst[:, half:half + N], b, 1.0, row[:, half:half + N], ALU.add, ALU.mult).then_inc(freed_by_dve, 1)
                    if n == 3:
                        dve.wait_ge(freed_by_dve, job.freed)
                        wait_freed(dve, "mod1")
                        for t in range(T):
                            step(nc.vector.tensor_tensor(hnat[:, t, :], hnat[:, t, :], gs, ALU.mult))
                            nc.vector.tensor_tensor(hnat[:, t, :], hnat[:, t, :], sh, ALU.add).then_inc(h_ready, 1)
                    continue
                if name.startswith("hT") or name.startswith("mT"):
                    t, half = int(name[2]), int(name[3])
                    dve.wait_ge(full, job.index + 1)
                    nc.vector.tensor_copy(actT[:, 4 * half:4 * half + 4, P * t:P * t + P], b.rearrange("p (k s) -> p k s", k=4)).then_inc(freed_by_dve, 1)
                    continue
                if name[:2] in ("rq", "rk"):
                    i, t = "qk".index(name[1]), int(name[3])
                    dve.wait_ge(full, job.index + 1)
                    if T * i + t:
                        dve.wait_ge(rot_ready, T * i + t)
                    v = b.rearrange("p (h c) -> p h c", h=RH)
                    c1 = cos[:, t, :].unsqueeze(1).to_broadcast([P, RH, 64])
                    s1 = sin[:, t, :].unsqueeze(1).to_broadcast([P, RH, 64])
                    lo, hi = rot[:, t, i, :, 0:64], rot[:, t, i, :, 64:128]
                    step.mark(nc.vector.tensor_tensor(lo, v[:, :, 0:64], c1, ALU.mult))
                    step.mark(nc.vector.tensor_tensor(hi, v[:, :, 0:64], s1, ALU.mult))
                    step.mark(nc.vector.tensor_tensor(rtmp[:, 0], v[:, :, 64:128], s1, ALU.mult))
                    nc.vector.tensor_tensor(rtmp[:, 1], v[:, :, 64:128], c1, ALU.mult).then_inc(freed_by_dve, 1)
                    step.sync()
                    dve.wait_ge(freed_by_dve, job.freed)
                    step.mark(nc.vector.tensor_tensor(lo, lo, rtmp[:, 0], ALU.subtract))
                    nc.vector.tensor_tensor(hi, hi, rtmp[:, 1], ALU.add).then_inc(rot_ready, 1)
                    continue
                if name.startswith("rs"):
                    u = int(name[2:])
                    h, t = units[u]
                    dve.wait_ge(full, job.index + 1)
                    src = b[:, 0:P * (t + 1)].rearrange("p (j s) -> p j s", j=t + 1)
                    nc.vector.tensor_tensor(sT[:, u % 2, 0:t + 1, :], src, decay[:, 0:t + 1, h, :], ALU.mult).then_inc(freed_by_dve, 1)
                    continue
                if name.startswith("ry"):
                    u = int(name[2:])
                    h, t = units[u]
                    dve.wait_ge(full, job.index + 1)
                    step.mark(nc.vector.bn_stats(stats[:, u % RH, :], b[:, 0:RDV]))
                    step.sync()
                    step.mark(nc.vector.bn_aggr(M["mv8"][:, u, :], stats[:, u % RH, :]))
                    nc.vector.tensor_copy(ynat[:, t, RDV * h:RDV * h + RDV], b[:, 0:RDV]).then_inc(freed_by_dve, 1)
                    if u == 7:
                        step.sync()
                        dve.wait_ge(freed_by_dve, job.freed)
                        nc.vector.tensor_scalar(M["var8"], M["mv8"][:, :, 1], GN_EPS, None, ALU.add).then_inc(var_ready, 1)
                        dve.wait_ge(ret_root_ready, 1)
                        step(nc.vector.reciprocal(M["var8"], M["var8"]))
                        wait_freed(dve, "rg1t1")
                        for v, (h, t) in enumerate(units):
                            y = ynat[:, t, RDV * h:RDV * h + RDV]
                            step.mark(nc.vector.tensor_scalar(y, y, M["mv8"][:, v, 0:1], M["var8"][:, v:v + 1], ALU.subtract, ALU.mult))
                        step.sync()
                        for t in range(T):
                            nc.vector.tensor_tensor(rg[:, t, :], rg[:, t, :], ynat[:, t, :], ALU.mult).then_inc(ret_ready, 1)
                    continue
                if name.startswith("ao"):
                    u = int(name[2:])
                    h, t = units[u]
                    dve.wait_ge(full, job.index + 1)
                    nc.vector.tensor_copy(attT[:, h, P * t:P * t + P], b[:, 0:P]).then_inc(freed_by_dve, 1)
                    continue
                half, t = int(name[2]), int(name[4])
                cols = slice(N * half, N * half + N)
                dve.wait_ge(full, job.index + 1)
                if name.startswith("ro"):
                    wait_freed(dve, f"ga{half}t{t}")
                    nc.vector.tensor_tensor(sga[:, t, cols], sga[:, t, cols], b, ALU.mult).then_inc(freed_by_dve, 1)
                elif name.startswith("to"):
                    wait_freed(dve, f"gb{half}t{t}")
                    nc.vector.tensor_tensor(sgb[:, t, cols], sgb[:, t, cols], b, ALU.mult).then_inc(freed_by_dve, 1)
                    dve.wait_ge(freed_by_dve, job.freed)
                    nc.vector.tensor_tensor(sga[:, t, cols], sga[:, t, cols], sgb[:, t, cols], ALU.add).then_inc(merged_ready, 1)
                elif name.startswith("wo"):
                    wait_freed(dve, "mod5")
                    nc.vector.tensor_tensor(sgb[:, t, cols], b, rows_mod[:, 0, cols], ALU.mult).then_inc(freed_by_dve, 1)
                    dve.wait_ge(freed_by_dve, job.freed)
                    nc.vector.tensor_tensor(x_sb[:, t, cols], x_sb[:, t, cols], sgb[:, t, cols], ALU.add).then_inc(x_ready, 1)
            dve.wait_ge(x_ready, 2 * T)

        @block.tensor
        def _(pe):
            ones, anti = const(M, "ones"), const(M, "anti")
            pe.wait_ge(const_here, 16)
            pe.wait_ge(tiny_here, 32)

            def product(out, lhs, job, t, chunks=KC):
                for k in range(chunks):
                    q = job.slots[k // 4]
                    if k % 4 == 0:
                        here(q)
                    w = ring[:, (q % slots_in_ring) * SLOT + N * (k % 4):(q % slots_in_ring) * SLOT + N * (k % 4) + N]
                    last = nc.tensor.matmul(out, lhs[:, k, P * t:P * t + P], w, start=k == 0, stop=k == chunks - 1)
                return last

            def here(q):
                pe.wait_ge(slot_here[q % slots_in_ring], 16 * (q // slots_in_ring + 1))

            for job in jobs.list:
                name, b = job.name, bank[job.index % BANKS]
                if job.index >= BANKS:
                    before = jobs.list[job.index - BANKS]
                    pe.wait_ge(freed[before.by], before.freed)
                if name == "cT":
                    last = nc.tensor.transpose(b[:, 0:KC], c8[:, :], ident[0:KC, 0:KC])
                elif name.startswith("tab"):
                    g = int(name[3:])
                    if g == 0:
                        pe.wait_ge(rel_ready, 1)
                        pe.wait_ge(rel_here, 32)
                    last = nc.tensor.matmul(b[0:AH, 0:TAB], bias_rel[:, AH * g:AH * g + AH], onehot[:, g, :], start=True, stop=True)
                elif name.startswith("ada"):
                    g = int(name[3:])
                    if g == 0:
                        pe.wait_ge(csb_ready, 1)
                    for k in range(KC):
                        here(job.slots[k])
                        at = (job.slots[k] % slots_in_ring) * SLOT
                        for j in range(4):
                            nc.tensor.matmul(b[32 * j:32 * j + 32, :], csb[:, k, :], ring[:, at + N * j:at + N * j + N], start=k == 0, stop=False)
                    for j in range(4):
                        pick = ident[0:12, 4 * g + j:4 * g + j + 1].to_broadcast([12, 32])
                        last = nc.tensor.matmul(b[32 * j:32 * j + 32, :], pick, b12[:, :], start=False, stop=True)
                elif name.startswith("mod"):
                    n = int(name[3:])
                    wait_freed(pe, f"ada{n // 4}")
                    r = 32 * (n % 4)
                    last = nc.tensor.matmul(b, ones[r:r + 1, :], mod4[r:r + 1, :], start=True, stop=True)
                elif name.startswith("hT") or name.startswith("mT"):
                    t, half = int(name[2]), int(name[3])
                    if name[0] == "h":
                        pe.wait_ge(h_ready, t + 1)
                    else:
                        pe.wait_ge(merged_ready, 2 * T)
                    src = hnat if name[0] == "h" else sga
                    for k in range(4):
                        last = nc.tensor.transpose(b[:, P * k:P * k + P], src[:, t, N * half + P * k:N * half + P * k + P], ident)
                elif name.startswith("rT"):
                    i, t = int(name[2]), int(name[3])
                    pe.wait_ge(rot_ready, T * i + t + 1)
                    for h in range(RH):
                        last = nc.tensor.transpose(b[:, P * h:P * h + P], rot[:, t, i, h, :], ident)
                elif name.startswith("retT"):
                    n = int(name[4])
                    pe.wait_ge(ret_ready, n // 2 + 1)
                    for k in range(4):
                        at = N * (n % 2) + P * k
                        last = nc.tensor.transpose(b[:, P * k:P * k + P], rg[:, n // 2, at:at + P], ident)
                elif name.startswith("rs"):
                    h, t = units[int(name[2:])]
                    wait_freed(pe, "rT11")
                    for back in range(t + 1):
                        j = t - back
                        last = nc.tensor.matmul(b[:, P * back:P * back + P], qkT[:, 1, h, P * j:P * j + P], qkT[:, 0, h, P * t:P * t + P], start=True, stop=True)
                elif name.startswith("ry"):
                    u = int(name[2:])
                    h, t = units[u]
                    wait_freed(pe, "rv1t1")
                    wait_freed(pe, f"rs{u}")
                    for back in range(t + 1):
                        last = nc.tensor.matmul(b[:, 0:RDV], sT[:, u % 2, back, :], rv[:, t - back, RDV * h:RDV * h + RDV], start=back == 0, stop=back == t)
                elif name[:2] in ("aq", "ak"):
                    h = int(name[2:]) % AH
                    for k in range(KC):
                        q = job.slots[k // 4]
                        if k % 4 == 0:
                            here(q)
                        at = (q % slots_in_ring) * SLOT + N * (k % 4) + P * h
                        last = nc.tensor.matmul(b[:, 0:S], ring[:, at:at + P], actT[:, k, :], start=k == 0, stop=k == KC - 1)
                elif name[:2] in ("sa", "sb"):
                    u = int(name[2:])
                    h, t = units[u]
                    w = P * (t + 1)
                    if u == 0:
                        pe.wait_ge(bias_here, 16 * AG)
                    wait_freed(pe, "ak11")
                    for g in ((0, 1) if name[1] == "a" else (2,)):
                        out = b[:, S * (g % 2):S * (g % 2) + w]
                        nc.tensor.matmul(out, aqT[:, AH * g + h, P * t:P * t + P], akT[:, AH * g + h, 0:w], start=True, stop=False)
                        last = nc.tensor.matmul(out, anti, hankel[:, g, h, S - w:S], start=False, stop=True)
                elif name.startswith("pT"):
                    u, n = int(name[2:-1]), int(name[-1])
                    pe.wait_ge(probs_ready, u + 1)
                    for g in range(AG):
                        last = nc.tensor.transpose(b[:, P * g:P * g + P], probs[:, u % 2, g, P * n:P * n + P], ident)
                elif name.startswith("ao"):
                    u = int(name[2:])
                    h, t = units[u]
                    wait_freed(pe, "av2t1")
                    wait_freed(pe, f"pT{u}{t}")
                    for n in range(t + 1):
                        for g in range(AG):
                            at = (AH * g + h) * ADH
                            last = nc.tensor.matmul(b[:, 0:P], av[:, n, at:at + ADH], probsT[:, u % 2, AG * n + g, :],
                                                    start=n + g == 0, stop=n == t and g == AG - 1)
                else:
                    lhs, t = actT, int(name.split("t")[-1])
                    if name == "rqt0":
                        wait_freed(pe, "hT10")
                        wait_freed(pe, "hT11")
                    elif name.startswith("ro"):
                        lhs = retT
                        wait_freed(pe, "retT3")
                    elif name.startswith("to"):
                        lhs = attT
                        wait_freed(pe, "ao7")
                    elif name.startswith("wo"):
                        wait_freed(pe, "mT10")
                        wait_freed(pe, "mT11")
                    last = product(b, lhs, job, t, 4 if name.startswith("to") else KC)
                last.then_inc(full, 1)


def experts(nc, M, A):
    x_sb, actT, ring, arena, psum = M["x"], M["actT"], M["ring"], M["arena"], M["psum"]
    bank, small = M["bank"], M["small"]
    hn = free(arena, 0, T, D)
    b1 = arena[0:E, 2048:4096]
    b2 = arena[0:E, 4096:5120]
    wr = free(arena, 5120, KC, E)
    br = free(arena, 5376, E)
    g_fin = free(arena, 6144, D)
    rows_mod = free(arena, 8192, 4, D)
    pick = free(arena, 12288, T, CAP)
    gated = free(arena, 12416, T, P)
    xg = free(arena, 12672, KC, CAP)
    glu, sig, lin, act_out = (free(arena, 13184 + N * i, N) for i in range(4))
    aT = free(arena, 15232, 4, P)
    gatedT = free(arena, 15744, T, P)
    y_sb = free(arena, 16000, N)
    zeros = free(arena, 16512, N)
    logits = free(arena, 17024, T, E)
    hit = free(arena, 17088, T, 4, E)
    weighed = free(arena, 17344, T, 4, E)
    chosen = free(arena, 17600, T, E)
    gates = free(arena, 17664, T, E + 1)
    place = free(arena, 17730, T, E + 1)
    own = arena[0:E, 17796:17796 + CAP]
    sumsq, rstd = small[:, 0:2], small[:, 2:4]
    top, gate4, first = free(small, 8, T, 8), free(small, 24, T, 4), free(small, 32, T, 8)
    negtop, gsum, most = small[:, 48:50], small[:, 50:52], small[:, 52:53]
    index, flags = M["index"], M["flags"]
    ident, ones, before = const(M, "ident"), const(M, "ones"), const(M, "before")
    numbers = const(M, "slots", ROUNDS, P)
    U, BU, BY, BG = psum[:, 4 * N:6 * N], 4, 6, 7
    UP, DOWN = KC, 4
    W = UP + DOWN

    jobs = Jobs(BANKS, [])
    for t in range(T):
        for half in range(2):
            jobs.add(f"hT{t}{half}", "act" if half else "dve")
    for t in range(T):
        jobs.add(f"lg{t}", "dve")
    for t in range(T):
        jobs.add(f"pl{t}", "dve")
    jobs.add("count", "dve")

    ctx = ExitStack()
    with ctx:
        def sem(name):
            return ctx.enter_context(nc.semaphore("moe_" + name))

        full, freed_by_act, freed_by_dve = sem("full"), sem("freed_by_act"), sem("freed_by_dve")
        freed = {"act": freed_by_act, "dve": freed_by_dve}
        slot_here = [sem(f"slot_here{k}") for k in range(W)]
        slot_used = sem("slot_used")
        row_here, fin_here, bias_here = sem("row_here"), sem("fin_here"), sem("bias_here")
        step_sem, zero_ready, pads_ready = sem("dve_step"), sem("zero_ready"), sem("pads_ready")
        squares_ready, mean_ready, root_ready, h_ready = sem("squares_ready"), sem("mean_ready"), sem("root_ready"), sem("h_ready")
        negtop_ready, exp_ready, chosen_ready, flags_ready = sem("negtop_ready"), sem("exp_ready"), sem("chosen_ready"), sem("flags_ready")
        own_ready, gated_ready, picked, gathered, xg_ready = sem("own_ready"), sem("gated_ready"), sem("picked"), sem("gathered"), sem("xg_ready")
        glu_ready, sig_ready, a_ready, aT_full, aT_ready = sem("glu_ready"), sem("sig_ready"), sem("a_ready"), sem("aT_full"), sem("aT_ready")
        lin_ready, prod_ready = sem("lin_ready"), sem("prod_ready")
        gatedT_full, gatedT_ready, y_ready, sums_done = sem("gatedT_full"), sem("gatedT_ready"), sem("y_ready"), sem("sums_done")
        x_ready, out_ready = sem("x_ready"), sem("out_ready")
        block = ctx.enter_context(nc.Block())

        def wait_freed(eng, name):
            job = jobs.by_name[name]
            eng.wait_ge(freed[job.by], job.freed)

        def further_rounds(eng, one_round):
            eng.wait_ge(flags_ready, 1)
            with eng.Fori(1, ROUNDS) as r:
                flag = eng.value_load(flags[0:1, bass.ds(r, 1)], min_val=0, max_val=1)
                with eng.If(flag == 1):
                    one_round(r)
                eng.nop()

        @block.sync
        def _(sp):
            def weights(e):
                for k in range(UP):
                    yield k, ring[:, SLOT * k:SLOT * (k + 1)], A["w_mlp1"][0, bass.ds(e, 1), P * k:P * (k + 1), :].rearrange("o p n -> p (o n)")
                for k in range(DOWN):
                    dst = ring[:, SLOT * (UP + k):SLOT * (UP + k + 1)].rearrange("p (k n) -> p k n", k=2)
                    yield UP + k, dst, A["w_mlp2"][0, bass.ds(e, 1), 2 * P * k:2 * P * (k + 1), :].rearrange("o (k p) n -> p (o k) n", p=P)

            sp.dma_start(wr, A["w_router"][0].rearrange("(k p) e -> p k e", p=P)).then_inc(row_here, 16)
            sp.dma_start(br.unsqueeze(1), A["b_router"][0:1, :].partition_broadcast(P)).then_inc(row_here, 16)
            sp.dma_start(b1, A["b_mlp1"][0]).then_inc(bias_here, 16)
            sp.dma_start(b2, A["b_mlp2"][0]).then_inc(bias_here, 16)
            sp.dma_start(g_fin.unsqueeze(1), A["g_final"].rearrange("(o d) -> o d", o=1).partition_broadcast(P)).then_inc(fin_here, 16)
            for k, dst, src in weights(0):
                sp.dma_start(dst, src).then_inc(slot_here[k], 16)

            def experts_from(r, first):
                with sp.Fori(first, E) as e:
                    for k, dst, src in weights(e):
                        sp.wait_ge(slot_used, (r * E + e - 1) * W + k + 1)
                        sp.dma_start(dst, src).then_inc(slot_here[k], 16)

            experts_from(0, 1)
            further_rounds(sp, lambda r: experts_from(r, 0))

        @block.scalar
        def _(act):
            for t in range(T):
                nc.scalar.activation(hn[:, t, :], x_sb[:, t, :], ACT.Square, accum_out=sumsq[:, t:t + 1]).then_inc(squares_ready, 1)
            act.wait_ge(mean_ready, 1)
            nc.scalar.activation(rstd, rstd, ACT.Sqrt).then_inc(root_ready, 1)
            for t in range(T):
                act.wait_ge(full, jobs.full(f"hT{t}1"))
                nc.scalar.copy(actT[:, 4:8, P * t:P * t + P], bank[jobs.bank(f"hT{t}1")].rearrange("p (k s) -> p k s", k=4)).then_inc(freed_by_act, 1)
            for t in range(T):
                act.wait_ge(negtop_ready, t + 1)
                nc.scalar.activation(gate4[:, t, :], top[:, t, 0:4], ACT.Exp, bias=negtop[:, t:t + 1], accum_out=gsum[:, t:t + 1]).then_inc(exp_ready, 1)
            act.nop().then_inc(aT_ready, 1)
            act.nop().then_inc(y_ready, 1)

            def gather_out(r, e):
                act.wait_ge(gathered, r * (E + 1) + e + 1)
                nc.scalar.copy(xg, bank[BG].rearrange("p (k s) -> p k s", k=KC)).then_inc(xg_ready, 1)

            def one_round(r):
                gather_out(r, 0)
                with act.Fori(0, E) as e:
                    i = r * E + e
                    act.wait_ge(gatedT_full, i + 1)
                    nc.scalar.copy(gatedT, bank[BY][:, 0:T * P].rearrange("p (t s) -> p t s", t=T)).then_inc(gatedT_ready, 1)
                    act.wait_ge(glu_ready, i + 1)
                    nc.scalar.activation(sig, glu, ACT.Sigmoid, scale=SWISH).then_inc(sig_ready, 1)
                    gather_out(r, e + 1)
                    act.wait_ge(aT_full, i + 1)
                    nc.scalar.copy(aT, bank[BU].rearrange("p (k s) -> p k s", k=4)).then_inc(aT_ready, 1)
                    act.wait_ge(slot_used, (i + 1) * W)
                    nc.scalar.copy(y_sb, bank[BY]).then_inc(y_ready, 1)

            one_round(0)
            further_rounds(act, one_round)
            for t in range(T):
                act.wait_ge(x_ready, 2 * (t + 1))
                nc.scalar.activation(hn[:, t, :], x_sb[:, t, :], ACT.Square, accum_out=sumsq[:, t:t + 1]).then_inc(squares_ready, 1)
            act.wait_ge(mean_ready, 2)
            nc.scalar.activation(rstd, rstd, ACT.Sqrt).then_inc(root_ready, 1)

        @block.vector
        def _(dve):
            step = Chain(dve, step_sem)
            nc.vector.memset(zeros, 0.0).then_inc(zero_ready, 1)
            step.mark(nc.vector.memset(gates[:, :, E:E + 1], 0.0))
            step.mark(nc.vector.memset(place[:, :, E:E + 1], -1.0))
            dve.wait_ge(squares_ready, T)
            nc.vector.tensor_scalar(rstd, sumsq, 1.0 / D, EPS, ALU.mult, ALU.add).then_inc(mean_ready, 1)
            dve.wait_ge(root_ready, 1)
            step(nc.vector.reciprocal(rstd, rstd))
            for t in range(T):
                step(nc.vector.scalar_tensor_tensor(hn[:, t, :], x_sb[:, t, :], rstd[:, t:t + 1], rows_mod[:, 2, :], ALU.mult, ALU.mult))
                nc.vector.tensor_tensor(hn[:, t, :], hn[:, t, :], rows_mod[:, 1, :], ALU.add).then_inc(h_ready, 1)
            for t in range(T):
                dve.wait_ge(full, jobs.full(f"hT{t}0"))
                nc.vector.tensor_copy(actT[:, 0:4, P * t:P * t + P], bank[jobs.bank(f"hT{t}0")].rearrange("p (k s) -> p k s", k=4)).then_inc(freed_by_dve, 1)
            dve.wait_ge(row_here, 32)
            for t in range(T):
                dve.wait_ge(full, jobs.full(f"lg{t}"))
                nc.vector.tensor_tensor(logits[:, t, :], bank[jobs.bank(f"lg{t}")][:, 0:E], br, ALU.add).then_inc(freed_by_dve, 1)
                wait_freed(dve, f"lg{t}")
                step(nc.vector.max(top[:, t, :], logits[:, t, :]))
                nc.vector.tensor_scalar(negtop[:, t:t + 1], top[:, t, 0:1], -1.0, None, ALU.mult).then_inc(negtop_ready, 1)
                step(nc.vector.max_index(index[:, t, :], top[:, t, :], logits[:, t, :]))
                step(nc.vector.tensor_copy(first[:, t, :], index[:, t, :]))
                for j in range(4):
                    step.mark(nc.vector.tensor_scalar(hit[:, t, j, :], numbers[:, 0, 0:E], first[:, t, j:j + 1], None, ALU.is_equal))
                step.sync()
                nc.vector.tensor_reduce(chosen[:, t, :], hit[:, t].rearrange("p j e -> p e j"), AX.X, ALU.add).then_inc(chosen_ready, 1)
            for t in range(T):
                dve.wait_ge(exp_ready, t + 1)
                step(nc.vector.reciprocal(gsum[:, t:t + 1], gsum[:, t:t + 1]))
                for j in range(4):
                    step.mark(nc.vector.tensor_scalar(weighed[:, t, j, :], hit[:, t, j, :], gate4[:, t, j:j + 1], gsum[:, t:t + 1], ALU.mult, ALU.mult))
                step.sync()
                step(nc.vector.tensor_reduce(gates[:, t, 0:E], weighed[:, t].rearrange("p j e -> p e j"), AX.X, ALU.add))
            for t in range(T):
                dve.wait_ge(full, jobs.full(f"pl{t}"))
                dve.wait_ge(chosen_ready, t + 1)
                nc.vector.scalar_tensor_tensor(place[:, t, 0:E], bank[jobs.bank(f"pl{t}")][:, 0:E], 1.0, chosen[:, t, :], ALU.add, ALU.mult).then_inc(freed_by_dve, 1)
                wait_freed(dve, f"pl{t}")
                step(nc.vector.tensor_scalar(place[:, t, 0:E], place[:, t, 0:E], -1.0, None, ALU.add))
            dve.wait_ge(full, jobs.full("count"))
            nc.vector.tensor_reduce(most, bank[jobs.bank("count")][:, 0:E], AX.X, ALU.max).then_inc(freed_by_dve, 1)
            wait_freed(dve, "count")
            nc.vector.tensor_scalar(flags[0:1, :], numbers[0:1, :, 0], most[0:1, :], None, ALU.is_lt).then_inc(flags_ready, 1)

            def choose(r, e):
                nc.vector.tensor_tensor(pick, numbers[:, bass.ds(r, 1), 0:CAP].to_broadcast([P, T, CAP]),
                                        place[:, :, bass.ds(e, 1)].to_broadcast([P, T, CAP]), ALU.is_equal).then_inc(picked, 1)

            def one_round(r):
                if not isinstance(r, int):
                    dve.wait_ge(gathered, r * (E + 1))
                choose(r, 0)
                with dve.Fori(0, E) as e:
                    i = r * E + e
                    dve.wait_ge(y_ready, i + 1)
                    nc.vector.tensor_copy(own, ident[0:E, bass.ds(e, 1)].to_broadcast([E, CAP])).then_inc(own_ready, 1)
                    for t in range(T):
                        nc.vector.scalar_tensor_tensor(gated[:, t, :], numbers[:, bass.ds(r, 1), :].rearrange("p o s -> p (o s)"), place[:, t, bass.ds(e, 1)],
                                                       gates[:, t, bass.ds(e, 1)].to_broadcast([P, P]), ALU.is_equal, ALU.mult).then_inc(gated_ready, 1)
                    dve.wait_ge(gathered, r * (E + 1) + e + 1)
                    choose(r, e + 1)
                    dve.wait_ge(slot_used, i * W + UP)
                    both = U.rearrange("p (n two) -> p n two", two=2)
                    nc.vector.tensor_scalar(glu, both[:, :, 0], LIMIT, None, ALU.min).then_inc(glu_ready, 1)
                    nc.vector.tensor_scalar(lin, both[:, :, 1], LIMIT, -LIMIT, ALU.min, ALU.max).then_inc(lin_ready, 1)
                    dve.wait_ge(lin_ready, i + 1)
                    dve.wait_ge(glu_ready, i + 1)
                    nc.vector.scalar_tensor_tensor(lin, lin, 1.0, glu, ALU.add, ALU.mult).then_inc(prod_ready, 1)
                    dve.wait_ge(prod_ready, i + 1)
                    dve.wait_ge(sig_ready, i + 1)
                    nc.vector.tensor_tensor(act_out, lin, sig, ALU.mult).then_inc(a_ready, 1)

            one_round(0)
            further_rounds(dve, one_round)
            dve.wait_ge(sums_done, 1)
            for t in range(T):
                for half in range(2):
                    cols = slice(N * half, N * half + N)
                    step(nc.vector.tensor_tensor(hn[:, t, cols], bank[2 * t + half], rows_mod[:, 3, cols], ALU.mult))
                    nc.vector.tensor_tensor(x_sb[:, t, cols], x_sb[:, t, cols], hn[:, t, cols], ALU.add).then_inc(x_ready, 1)
            dve.wait_ge(squares_ready, 2 * T)
            nc.vector.tensor_scalar(rstd, sumsq, 1.0 / D, EPS, ALU.mult, ALU.add).then_inc(mean_ready, 1)
            dve.wait_ge(root_ready, 2)
            step(nc.vector.reciprocal(rstd, rstd))
            dve.wait_ge(fin_here, 16)
            for t in range(T):
                nc.vector.scalar_tensor_tensor(x_sb[:, t, :], x_sb[:, t, :], rstd[:, t:t + 1], g_fin, ALU.mult, ALU.mult).then_inc(out_ready, 1)

        @block.tensor
        def _(pe):
            def start(name):
                job = jobs.by_name[name]
                if job.index >= BANKS:
                    before_it = jobs.list[job.index - BANKS]
                    pe.wait_ge(freed[before_it.by], before_it.freed)
                return bank[job.index % BANKS]

            for t in range(T):
                pe.wait_ge(h_ready, t + 1)
                for half in range(2):
                    b = start(f"hT{t}{half}")
                    for k in range(4):
                        at = N * half + P * k
                        last = nc.tensor.transpose(b[:, P * k:P * k + P], hn[:, t, at:at + P], ident)
                    last.then_inc(full, 1)
            pe.wait_ge(row_here, 32)
            for t in range(T):
                wait_freed(pe, f"hT{t}0")
                wait_freed(pe, f"hT{t}1")
                b = start(f"lg{t}")
                for k in range(KC):
                    last = nc.tensor.matmul(b[:, 0:E], actT[:, k, P * t:P * t + P], wr[:, k, :], start=k == 0, stop=k == KC - 1)
                last.then_inc(full, 1)
            for t in range(T):
                pe.wait_ge(chosen_ready, t + 1)
                b = start(f"pl{t}")
                for j in range(t + 1):
                    last = nc.tensor.matmul(b[:, 0:E], before if j == t else ones, chosen[:, j, :], start=j == 0, stop=j == t)
                last.then_inc(full, 1)
            b = start("count")
            for j in range(T):
                last = nc.tensor.matmul(b[:, 0:E], ones, chosen[:, j, :], start=j == 0, stop=j == T - 1)
            last.then_inc(full, 1)
            wait_freed(pe, "count")
            pe.wait_ge(zero_ready, 1)
            for n in range(4):
                nc.tensor.matmul(bank[n], zeros[:, 0:P], zeros, start=True, stop=False)

            def gather(r, e):
                pe.wait_ge(picked, r * (E + 1) + e + 1)
                for k in range(KC):
                    for t in range(T):
                        last = nc.tensor.matmul(bank[BG][:, CAP * k:CAP * k + CAP], hn[:, t, P * k:P * k + P], pick[:, t, :], start=t == 0, stop=t == T - 1)
                last.then_inc(gathered, 1)

            def one_round(r):
                if not isinstance(r, int):
                    pe.wait_ge(xg_ready, r * (E + 1))
                gather(r, 0)
                with pe.Fori(0, E) as e:
                    i = r * E + e
                    pe.wait_ge(xg_ready, r * (E + 1) + e + 1)
                    pe.wait_ge(own_ready, i + 1)
                    pe.wait_ge(aT_ready, i + 1)
                    for n in range(2):
                        for h in range(2):
                            nc.tensor.matmul(U[CAP * h:CAP * h + CAP, N * n:N * n + N], own, b1[:, 2 * N * h + N * n:2 * N * h + N * n + N], start=True, stop=False)
                    for k in range(UP):
                        pe.wait_ge(slot_here[k], (i + 1) * 16)
                        for n in range(2):
                            for h in range(2):
                                at = SLOT * k + 2 * N * h + N * n
                                last = nc.tensor.matmul(U[CAP * h:CAP * h + CAP, N * n:N * n + N], xg[:, k, :], ring[:, at:at + N], start=False, stop=k == UP - 1)
                        last.then_inc(slot_used, 1)
                    pe.wait_ge(gated_ready, (i + 1) * T)
                    for t in range(T):
                        last = nc.tensor.transpose(bank[BY][:, P * t:P * t + P], gated[:, t, :], ident)
                    last.then_inc(gatedT_full, 1)
                    gather(r, e + 1)
                    pe.wait_ge(a_ready, i + 1)
                    for k in range(4):
                        last = nc.tensor.transpose(bank[BU][:, P * k:P * k + P], act_out[:, P * k:P * k + P], ident)
                    last.then_inc(aT_full, 1)
                    pe.wait_ge(gatedT_ready, i + 1)
                    for h in range(2):
                        nc.tensor.matmul(bank[BY][CAP * h:CAP * h + CAP, :], own, b2[:, N * h:N * h + N], start=True, stop=False)
                    pe.wait_ge(aT_ready, i + 2)
                    for k in range(KC):
                        if k % 2 == 0:
                            pe.wait_ge(slot_here[UP + k // 2], (i + 1) * 16)
                        for h in range(2):
                            at = SLOT * UP + D * k + N * h
                            last = nc.tensor.matmul(bank[BY][CAP * h:CAP * h + CAP, :], aT[:, k % 4, CAP * (k // 4):CAP * (k // 4) + CAP], ring[:, at:at + N], start=False, stop=k == KC - 1)
                        if k % 2:
                            last.then_inc(slot_used, 1)
                    pe.wait_ge(y_ready, i + 2)
                    for t in range(T):
                        for h in range(2):
                            nc.tensor.matmul(bank[2 * t + h], gatedT[CAP * h:CAP * h + CAP, t, :], y_sb[CAP * h:CAP * h + CAP, :], start=False, stop=False)

            pe.wait_ge(bias_here, 32)
            one_round(0)
            further_rounds(pe, one_round)
            for n in range(4):
                last = nc.tensor.matmul(bank[n], zeros[:, 0:P], zeros, start=False, stop=True)
            last.then_inc(sums_done, 1)


def layer(nc, M, A, i, out=None):
    x_sb, actT, ring, arena, bank, small = M["x"], M["actT"], M["ring"], M["arena"], M["bank"], M["small"]
    WIDE = 256
    QK = W_MIX // P
    memT = free(arena, 0, KC, N_MEM)
    rows = free(arena, 2048, 4, D)
    catT = free(arena, 6144, KC, S)
    kmT, vm, qmT = free(arena, 8192, 2, N_MEM), free(arena, 8704, 2, W_MEM), free(arena, 9216, 2, S)
    u_nat, v_nat, wsT, ws = free(arena, 9728, T, W_MIX), free(arena, 11264, T, W_MIX), free(arena, 12800, HEADS, P), free(arena, 14336, HEADS, P)
    v_rows = free(arena, 15872, 2, W_MIX)
    qT, kT, v_self = free(arena, 9728, QK, S), free(arena, 11264, QK, S), free(arena, 12800, T, W_MIX)
    mem_nat = free(arena, 17408, T, D)
    probs = free(arena, 17408, 2, 4, S)
    probsT = free(arena, 19456, 2, 4, P)
    hidden = free(arena, 9728, FC2, S)
    silu = free(arena, 15360, 2, N)
    stats, mv, root = free(small, 0, T, 3, 6), free(small, 36, T, 2), small[:, 40:42]
    bsT, negmax, lsum = small[:, 44:56], free(small, 56, 2, 4), free(small, 64, 2, 4)
    bs = M["b12"][:, 0:P]
    ident, upto, causal = const(M, "ident"), const(M, "upto"), const(M, "causal")

    slots = []

    def wide(w, col):
        slots.append(w[:, col:col + WIDE].rearrange("(k p) n -> p k n", p=P))
        return [len(slots) - 1]

    def half_columns(w, col):
        first, n = len(slots), w.shape[0] // P
        for k in range(0, n, 4):
            m = min(4, n - k)
            slots.append(w[P * k:P * (k + m), col:col + N].rearrange("(k p) n -> p k n", p=P))
        return list(range(first, len(slots)))

    jobs = Jobs(BANKS, slots)
    w_kv, w_in = A["w_mem_kv_2"][i], A["b_w_in_2" if i else "a_w_in_2"][0]
    units = [("mem", 0, t) for t in range(T)]
    if i:
        units += [("self", c, t) for c in range(3) for t in range(T)]

    def scores(u):
        by = "act" if units[u][0] == "mem" else "dve"
        jobs.add(f"sa{u}", by)
        jobs.add(f"sb{u}", by)

    def weights_over(u):
        kind, c, t = units[u]
        for n in range(2 if kind == "mem" else t + 1):
            jobs.add(f"pT{u}:{n}", "act")

    for t in range(T):
        for half in range(2):
            jobs.add(f"xT{t}{half}", "act" if half else "dve")
    if i == 0:
        for n in range(3):
            jobs.add(f"vn{n}", "act", wide(w_in, W_MIX + WIDE * n))
        for t in range(T):
            for half in range(2):
                jobs.add(f"memT{t}{half}", "dve" if half else "act")
        jobs.add("qm", "act", wide(w_in, 2 * W_MIX))
        jobs.add("km", "act", wide(w_kv, 0))
        jobs.add("vm", "act", wide(w_kv, W_MEM))
        for n in range(3):
            jobs.add(f"wsT{n}", "dve")
        jobs.add("bsT", "dve")
        scores(0)
        jobs.add("un0", "act", wide(w_in, 0))
        scores(1)
        weights_over(0)
        jobs.add("un1", "act", wide(w_in, WIDE))
        jobs.add("ao0", "dve")
        weights_over(1)
        jobs.add("un2", "act", wide(w_in, 2 * WIDE))
        jobs.add("ao1", "dve")
        for n in range(3):
            jobs.add(f"sv{n}", "dve")
        for n in range(3):
            jobs.add(f"mixT{n}", "act")
    else:
        jobs.add("qm", "act", wide(w_in, 3 * W_MIX))
        jobs.add("km", "act", wide(w_kv, 0))
        jobs.add("vm", "act", wide(w_kv, W_MEM))
        fill = [(f"{what}{n}", "act", at + WIDE * n) for n in range(3) for what, at in (("q_", 0), ("k_", W_MIX), ("v_", 2 * W_MIX))]

        def some():
            if fill:
                name, by, col = fill.pop(0)
                jobs.add(name, by, wide(w_in, col))

        scores(0)
        some()
        scores(1)
        some()
        weights_over(0)
        some()
        jobs.add("ao0", "dve")
        for u in range(2, len(units) + 1):
            if u < len(units):
                scores(u)
            some()
            weights_over(u - 1)
            if u % 2:
                some()
                some()
            jobs.add(f"ao{u - 1}", "dve")
        assert not fill
    for half in range(2):
        c = half_columns(A["w_mix_out_2"][i], N * half)
        for t in range(T):
            jobs.add(f"pr{half}t{t}", "dve", c)
    for t in range(T):
        for half in range(2):
            jobs.add(f"yT{t}{half}", "act" if half else "dve")
    w_ffn = A["w_ffn_in_2"][i]
    for n in range(F2 // WIDE):
        jobs.add(f"fg{n}", "act", wide(w_ffn, WIDE * n))
        jobs.add(f"fu{n}", "dve", wide(w_ffn, F2 + WIDE * n))
    for half in range(2):
        c = half_columns(A["w_ffn_out_2"][i], N * half)
        for t in range(T):
            jobs.add(f"fo{half}t{t}", "dve", c)

    ctx = ExitStack()
    with ctx:
        def sem(name):
            return ctx.enter_context(nc.semaphore(f"layer{i}_{name}"))

        full, freed_by_act, freed_by_dve = sem("full"), sem("freed_by_act"), sem("freed_by_dve")
        freed = {"act": freed_by_act, "dve": freed_by_dve}
        slot_here = [sem(f"slot_here{k}") for k in range(RING)]
        rows_here, mem_here, ws_here, v_rows_here, bs_here = sem("rows_here"), sem("mem_here"), sem("ws_here"), sem("v_rows_here"), sem("bs_here")
        step_sem, var_ready, root_ready, v_ready, mix_ready = sem("dve_step"), sem("var_ready"), sem("root_ready"), sem("v_ready"), sem("mix_ready")
        max_ready, exp_ready, probs_ready, x_ready, out_done = sem("max_ready"), sem("exp_ready"), sem("probs_ready"), sem("x_ready"), sem("out_done")
        block = ctx.enter_context(nc.Block())

        def wait_freed(eng, name):
            job = jobs.by_name[name]
            eng.wait_ge(freed[job.by], job.freed)

        @block.sync
        def _(sp):
            for q, src in enumerate(slots):
                if q >= RING:
                    sp.wait_ge(full, jobs.last_use[q - RING] + 1)
                k, n = src.shape[1], src.shape[2]
                at = (q % RING) * SLOT
                sp.dma_start(ring[:, at:at + k * n].rearrange("p (k n) -> p k n", n=n), src).then_inc(slot_here[q % RING], 16)
            if out is not None:
                for t in range(T):
                    sp.wait_ge(x_ready, T + t + 1)
                    sp.dma_start(out[0, P * t:P * t + P, :], x_sb[:, t, :]).then_inc(out_done, 16)
                sp.wait_ge(out_done, 16 * T)

        @block.gpsimd
        def _(pool):
            if i == 0:
                pool.dma_start(mem_nat, A["mem_2"][0].rearrange("(t p) d -> p t d", p=P)).then_inc(mem_here, 16)
                pool.dma_start(ws, A["a_w_s_2"][0].rearrange("g t s -> t g s")).then_inc(ws_here, 16)
                pool.dma_start(bs, A["a_b_s_2"][0]).then_inc(bs_here, 16)
                for n, name in enumerate(("a_ln_v_g_2", "a_ln_v_b_2")):
                    pool.dma_start(v_rows[:, n, :].unsqueeze(1), A[name][0:1, :].partition_broadcast(P)).then_inc(v_rows_here, 16)
            for n, name in enumerate(("ln_mix_g_2", "ln_mix_b_2", "ln_ffn_g_2", "ln_ffn_b_2")):
                pool.dma_start(rows[:, n, :].unsqueeze(1), A[name][i:i + 1, :].partition_broadcast(P)).then_inc(rows_here, 16)
            pool.wait_ge(rows_here, 64)

        @block.scalar
        def _(act):
            roots = [0]

            def take_root(t):
                roots[0] += 1
                act.wait_ge(var_ready, roots[0])
                nc.scalar.activation(root[:, t:t + 1], mv[:, t, 1:2], ACT.Sqrt).then_inc(root_ready, 1)

            for job in jobs.list:
                name, b = job.name, bank[job.index % BANKS]
                pair = b.rearrange("p (a s) -> p a s", a=2)
                if name[:2] in ("sa", "sb"):
                    u, part = int(name[2:]), "ab".index(name[1])
                    kind, c, t = units[u]
                    w = S if kind == "mem" else P * (t + 1)
                    act.wait_ge(max_ready, 2 * u + part + 1)
                    for n in range(2):
                        at = 2 * part + n
                        dst = probs[:, u % 2, at, 0:w]
                        last = nc.scalar.activation(dst, pair[:, n, :] if kind == "mem" else dst, ACT.Exp, bias=negmax[:, u % 2, at:at + 1], accum_out=lsum[:, u % 2, at:at + 1])
                        if n == 1 and kind == "mem":
                            last.then_inc(freed_by_act, 1)
                        elif n == 1:
                            last.then_inc(exp_ready, 1)
                    continue
                if job.by != "act":
                    if name.startswith("pr1t") or name.startswith("fo1t"):
                        take_root(int(name[4]))
                    continue
                if name == "memT00" and i == 0:
                    for t in range(T):
                        take_root(t)
                act.wait_ge(full, job.index + 1)
                if name.startswith("vn"):
                    n = int(name[2])
                    last = nc.scalar.activation(v_nat[:, :, WIDE * n:WIDE * n + WIDE], pair, ACT.Gelu_apprx_tanh)
                elif name.startswith("un"):
                    n = int(name[2])
                    last = nc.scalar.activation(u_nat[:, :, WIDE * n:WIDE * n + WIDE], pair, ACT.Gelu_apprx_tanh)
                elif name[:2] in ("xT", "yT"):
                    t, half = int(name[2]), int(name[3])
                    last = nc.scalar.copy(actT[:, 4 * half:4 * half + 4, P * t:P * t + P], b.rearrange("p (k s) -> p k s", k=4))
                elif name.startswith("memT"):
                    t, half = int(name[4]), int(name[5])
                    last = nc.scalar.copy(memT[:, 4 * half:4 * half + 4, P * t:P * t + P], b.rearrange("p (k s) -> p k s", k=4))
                elif name == "qm":
                    last = nc.scalar.mul(qmT, pair, DH ** -0.5)
                elif name == "km":
                    last = nc.scalar.copy(kmT, pair)
                elif name == "vm":
                    last = nc.scalar.copy(vm, pair)
                elif name.startswith("q_"):
                    n = int(name[2])
                    last = nc.scalar.mul(qT[:, 2 * n:2 * n + 2, :], pair, DH ** -0.5)
                elif name.startswith("k_"):
                    n = int(name[2])
                    last = nc.scalar.copy(kT[:, 2 * n:2 * n + 2, :], pair)
                elif name.startswith("v_"):
                    n = int(name[2])
                    last = nc.scalar.copy(v_self[:, :, WIDE * n:WIDE * n + WIDE], pair)
                elif name.startswith("pT"):
                    n = int(name.split(":")[1])
                    last = nc.scalar.copy(probsT[:, n], b.rearrange("p (h s) -> p h s", h=4))
                elif name.startswith("mixT"):
                    n = int(name[4])
                    last = nc.scalar.copy(catT[:, 2 * n:2 * n + 2, :], pair)
                elif name.startswith("fg"):
                    n = int(name[2:])
                    if n >= 2:
                        wait_freed(act, f"fu{n - 2}")
                    last = nc.scalar.activation(silu[:, n % 2, :], b, ACT.Silu)
                last.then_inc(freed_by_act, 1)

        @block.vector
        def _(dve):
            step = Chain(dve, step_sem)
            roots = [0]
            dve.wait_ge(rows_here, 64)

            def norm(t, pieces, v, g, b, ready):
                step(nc.vector.bn_aggr(mv[:, t, :], stats[:, t, 0:pieces, :]))
                nc.vector.tensor_scalar(mv[:, t, 1:2], mv[:, t, 1:2], LN_EPS, None, ALU.add).then_inc(var_ready, 1)
                step.mark(nc.vector.scalar_tensor_tensor(v, v, mv[:, t, 0:1], g, ALU.subtract, ALU.mult))
                roots[0] += 1
                dve.wait_ge(root_ready, roots[0])
                step(nc.vector.reciprocal(root[:, t:t + 1], root[:, t:t + 1]))
                nc.vector.scalar_tensor_tensor(v, v, root[:, t:t + 1], b, ALU.mult, ALU.add).then_inc(ready, 1)

            for job in jobs.list:
                name, b = job.name, bank[job.index % BANKS]
                pair = b.rearrange("p (a s) -> p a s", a=2)
                if name.startswith("vn"):
                    n = int(name[2])
                    wait_freed(dve, name)
                    for t in range(T):
                        step.mark(nc.vector.bn_stats(stats[:, t, n, :], v_nat[:, t, WIDE * n:WIDE * n + WIDE]))
                    if n == 2:
                        step.sync()
                        dve.wait_ge(v_rows_here, 32)
                        for t in range(T):
                            norm(t, 3, v_nat[:, t, :], v_rows[:, 0, :], v_rows[:, 1, :], v_ready)
                    continue
                if name[:2] in ("sa", "sb"):
                    u, part = int(name[2:]), "ab".index(name[1])
                    kind, c, t = units[u]
                    dve.wait_ge(full, job.index + 1)
                    src = pair
                    if kind == "self":
                        w = P * (t + 1)
                        src = probs[:, u % 2, 2 * part:2 * part + 2, 0:w]
                        mask = causal[:, S - w:S].unsqueeze(1).to_broadcast([P, 2, w])
                        nc.vector.tensor_tensor(src, pair[:, :, 0:w], mask, ALU.add).then_inc(freed_by_dve, 1)
                        dve.wait_ge(freed_by_dve, job.freed)
                    nc.vector.tensor_reduce(negmax[:, u % 2, 2 * part:2 * part + 2], src, AX.X, ALU.max, negate=True).then_inc(max_ready, 1)
                    continue
                if name.startswith("pT") and name.endswith(":0"):
                    u = int(name[2:-2])
                    kind, c, t = units[u]
                    w = S if kind == "mem" else P * (t + 1)
                    if kind == "mem":
                        wait_freed(dve, f"sb{u}")
                    else:
                        dve.wait_ge(exp_ready, 2 * (u - T) + 2)
                    step(nc.vector.reciprocal(lsum[:, u % 2, :], lsum[:, u % 2, :]))
                    pr = probs[:, u % 2, :, 0:w]
                    nc.vector.tensor_tensor(pr, pr, lsum[:, u % 2, :].unsqueeze(2).to_broadcast([P, 4, w]), ALU.mult).then_inc(probs_ready, 1)
                    continue
                if job.by != "dve":
                    continue
                dve.wait_ge(full, job.index + 1)
                if name[:2] in ("xT", "yT"):
                    t, half = int(name[2]), int(name[3])
                    nc.vector.tensor_copy(actT[:, 4 * half:4 * half + 4, P * t:P * t + P], b.rearrange("p (k s) -> p k s", k=4)).then_inc(freed_by_dve, 1)
                elif name.startswith("memT"):
                    t, half = int(name[4]), int(name[5])
                    nc.vector.tensor_copy(memT[:, 4 * half:4 * half + 4, P * t:P * t + P], b.rearrange("p (k s) -> p k s", k=4)).then_inc(freed_by_dve, 1)
                elif name.startswith("wsT"):
                    n = int(name[3])
                    nc.vector.tensor_tensor(wsT[:, 4 * n:4 * n + 4, :], b.rearrange("p (g s) -> p g s", g=4), upto.unsqueeze(1).to_broadcast([P, 4, P]), ALU.mult).then_inc(freed_by_dve, 1)
                elif name == "bsT":
                    nc.vector.tensor_copy(bsT, b[:, 0:HEADS]).then_inc(freed_by_dve, 1)
                elif name.startswith("sv"):
                    n = int(name[2])
                    wait_freed(dve, "bsT")
                    wait_freed(dve, "un2")
                    for j in range(4):
                        g = 4 * n + j
                        cols = u_nat[:, :, DH * g:DH * g + DH]
                        last = nc.vector.scalar_tensor_tensor(cols, b.rearrange("p (g c d) -> p g c d", g=4, c=T)[:, j], bsT[:, g:g + 1], cols, ALU.add, ALU.mult)
                    last.then_inc(freed_by_dve, 1)
                elif name.startswith("ao"):
                    u = int(name[2:])
                    kind, c, t = units[u]
                    at = QK if kind == "mem" else 2 * c
                    nc.vector.tensor_copy(catT[:, at:at + 2, P * t:P * t + P], b[:, 0:2 * P].rearrange("p (a s) -> p a s", a=2)).then_inc(freed_by_dve, 1)
                elif name[:2] in ("pr", "fo"):
                    half, t = int(name[2]), int(name[4])
                    cols = x_sb[:, t, N * half:N * half + N]
                    nc.vector.scalar_tensor_tensor(cols, cols, ALPHA, b, ALU.mult, ALU.add).then_inc(freed_by_dve, 1)
                    dve.wait_ge(freed_by_dve, job.freed)
                    step.mark(nc.vector.bn_stats(stats[:, t, half, :], cols))
                    if half:
                        step.sync()
                        r = 0 if name[0] == "p" else 2
                        norm(t, 2, x_sb[:, t, :], rows[:, r, :], rows[:, r + 1, :], x_ready)
                elif name.startswith("fu"):
                    n = int(name[2:])
                    wait_freed(dve, f"fg{n}")
                    nc.vector.tensor_tensor(hidden[:, 2 * n:2 * n + 2, :].rearrange("p a s -> p (a s)"), silu[:, n % 2, :], b, ALU.mult).then_inc(freed_by_dve, 1)

        @block.tensor
        def _(pe):
            def here(q):
                pe.wait_ge(slot_here[q % RING], 16 * (q // RING + 1))

            def natural(b, lhs, q):
                here(q)
                at = (q % RING) * SLOT
                for t in range(T):
                    for k in range(KC):
                        last = nc.tensor.matmul(b[:, WIDE * t:WIDE * t + WIDE], lhs[:, k, P * t:P * t + P], ring[:, at + WIDE * k:at + WIDE * (k + 1)], start=k == 0, stop=k == KC - 1)
                return last

            def transposed(b, rhs, q):
                here(q)
                for a in range(2):
                    for k in range(KC):
                        at = (q % RING) * SLOT + WIDE * k + P * a
                        last = nc.tensor.matmul(b[:, S * a:S * a + S], ring[:, at:at + P], rhs[:, k, :], start=k == 0, stop=k == KC - 1)
                return last

            for job in jobs.list:
                name, b = job.name, bank[job.index % BANKS]
                if job.index >= BANKS:
                    before = jobs.list[job.index - BANKS]
                    pe.wait_ge(freed[before.by], before.freed)
                if name[:2] in ("xT", "yT"):
                    t, half = int(name[2]), int(name[3])
                    if name[0] == "y":
                        pe.wait_ge(x_ready, t + 1)
                    for k in range(4):
                        at = N * half + P * k
                        last = nc.tensor.transpose(b[:, P * k:P * k + P], x_sb[:, t, at:at + P], ident)
                elif name.startswith("memT"):
                    t, half = int(name[4]), int(name[5])
                    pe.wait_ge(mem_here, 16)
                    for k in range(4):
                        at = N * half + P * k
                        last = nc.tensor.transpose(b[:, P * k:P * k + P], mem_nat[:, t, at:at + P], ident)
                elif name[:2] in ("vn", "un", "v_"):
                    if name == "vn0":
                        wait_freed(pe, "xT10")
                        wait_freed(pe, "xT11")
                    last = natural(b, actT, job.slots[0])
                elif name[:2] in ("q_", "k_") or name == "qm":
                    if name == "qm":
                        wait_freed(pe, "xT10")
                        wait_freed(pe, "xT11")
                    last = transposed(b, actT, job.slots[0])
                elif name == "km":
                    if i == 0:
                        wait_freed(pe, "memT10")
                        wait_freed(pe, "memT11")
                    last = transposed(b, memT, job.slots[0])
                elif name == "vm":
                    last = natural(b, memT, job.slots[0])
                elif name.startswith("wsT"):
                    n = int(name[3])
                    pe.wait_ge(ws_here, 16)
                    for j in range(4):
                        last = nc.tensor.transpose(b[:, P * j:P * j + P], ws[:, 4 * n + j, :], ident)
                elif name == "bsT":
                    pe.wait_ge(bs_here, 16)
                    last = nc.tensor.transpose(b[:, 0:HEADS], bs, ident[0:HEADS, 0:HEADS])
                elif name[:2] in ("sa", "sb"):
                    u, part = int(name[2:]), "ab".index(name[1])
                    kind, c, t = units[u]
                    q_, k_, at, w = (qmT, kmT, 0, S) if kind == "mem" else (qT, kT, 2 * c, P * (t + 1))
                    wait_freed(pe, "km" if kind == "mem" else f"k_{c}")
                    r = slice(DH * part, DH * part + DH)
                    for n in range(2):
                        last = nc.tensor.matmul(b[:, S * n:S * n + w], q_[r, at + n, P * t:P * t + P], k_[r, at + n, 0:w], start=True, stop=True)
                elif name.startswith("pT"):
                    u, n = (int(v) for v in name[2:].split(":"))
                    pe.wait_ge(probs_ready, u + 1)
                    for h in range(4):
                        last = nc.tensor.transpose(b[:, P * h:P * h + P], probs[:, u % 2, h, P * n:P * n + P], ident)
                elif name.startswith("ao"):
                    u = int(name[2:])
                    kind, c, t = units[u]
                    blocks = 2 if kind == "mem" else t + 1
                    wait_freed(pe, f"pT{u}:{blocks - 1}")
                    wait_freed(pe, "vm" if kind == "mem" else f"v_{c}")
                    v = vm if kind == "mem" else v_self
                    for n in range(2):
                        for part in range(2):
                            for m in range(blocks):
                                at = (0 if kind == "mem" else 4 * c * DH) + DH * (2 * n + part)
                                last = nc.tensor.matmul(b[DH * part:DH * part + DH, P * n:P * n + P], v[:, m, at:at + DH], probsT[:, m, 2 * part + n, :],
                                                        start=m == 0, stop=m == blocks - 1)
                elif name.startswith("sv"):
                    n = int(name[2])
                    pe.wait_ge(v_ready, T)
                    wait_freed(pe, f"wsT{n}")
                    for j in range(4):
                        g = 4 * n + j
                        last = nc.tensor.matmul(b[:, T * DH * j:T * DH * (j + 1)], wsT[:, g, :], v_nat[:, :, DH * g:DH * g + DH], start=True, stop=True)
                elif name.startswith("mixT"):
                    n = int(name[4])
                    wait_freed(pe, f"sv{n}")
                    for a in range(2):
                        for t in range(T):
                            last = nc.tensor.transpose(b[:, S * a + P * t:S * a + P * t + P], u_nat[:, t, P * (2 * n + a):P * (2 * n + a) + P], ident)
                elif name[:2] in ("fg", "fu"):
                    if name == "fg0":
                        wait_freed(pe, "yT10")
                        wait_freed(pe, "yT11")
                    last = transposed(b, actT, job.slots[0])
                elif name[:2] in ("pr", "fo"):
                    t = int(name[4])
                    if name[0] == "p":
                        lhs, chunks = catT, KC
                        wait_freed(pe, f"ao{len(units) - 1}")
                        if i == 0:
                            wait_freed(pe, "mixT2")
                    else:
                        lhs, chunks = hidden, FC2
                        wait_freed(pe, f"fu{F2 // WIDE - 1}")
                    for k in range(chunks):
                        q = job.slots[k // 4]
                        if k % 4 == 0:
                            here(q)
                        at = (q % RING) * SLOT + N * (k % 4)
                        last = nc.tensor.matmul(b, lhs[:, k, P * t:P * t + P], ring[:, at:at + N], start=k == 0, stop=k == chunks - 1)
                last.then_inc(full, 1)


def layers(nc, M, A, out):
    layer(nc, M, A, 0)
    layer(nc, M, A, 1, out)


def program(nc, A, out):
    scratch = nc.dram_tensor("bias_by_distance", (AG * AH, TAB), FP32, kind="Internal").ap()
    with ExitStack() as ctx:
        def sb(name, shape, dt=FP32):
            return ctx.enter_context(nc.sbuf_tensor(name, shape, dt))

        M = {
            "ring": sb("ring", [P, RING * SLOT]),
            "arena": sb("arena", [P, ARENA]),
            "x": sb("x_res", [P, T, D]),
            "actT": sb("actT", [P, KC, S]),
            "const": sb("consts", [P, CONST_W]),
            "small": sb("small", [P, 384]),
            "c8": sb("c8", [KC, P]),
            "b12": sb("b12", [12, N]),
            "mv8": sb("mv8", [P, RH * T, 2])[:, :, :],
            "var8": sb("var8", [P, RH * T])[:, :],
            "index": sb("index", [P, T, 8], mybir.dt.uint32),
            "flags": sb("flags", [1, ROUNDS], I32),
        }
        psum = ctx.enter_context(nc.psum_tensor("psum", [P, BANKS * N], FP32))
        M["psum"] = psum
        M["bank"] = [psum[:, N * n:N * n + N] for n in range(BANKS)]
        mixer(nc, M, A, scratch)
        experts(nc, M, A)
        layers(nc, M, A, out)


def kernel(**inputs):
    import numpy as _np
    import concourse.bacc as _bacc
    from concourse import mybir as _mybir
    from concourse.bass_utils import run_bass_kernel_spmd as _run

    nc = _bacc.Bacc("TRN2", target_bir_lowering=False, num_devices=1)
    arrays, A = {}, {}
    table, onehot = shape_constants()
    for name, a in [*inputs.items(), ("table", table), ("onehot", onehot)]:
        a = _np.ascontiguousarray(a)
        arrays[f"in_{name}_dram"] = a
        A[name] = nc.dram_tensor(f"in_{name}_dram", a.shape, _mybir.dt.from_np(a.dtype), kind="ExternalInput").ap()
    out = nc.dram_tensor("out_dram", (1, S, D), FP32, kind="ExternalOutput").ap()
    program(nc, A, out)
    r = _run(nc, [arrays], core_ids=[0])
    return r.results[0]["out_dram"]
```

```python
import math
from contextlib import ExitStack

import numpy as np

import concourse.bass as bass
from concourse import mybir

FP32 = mybir.dt.float32
F32R = mybir.dt.float32r
I32 = mybir.dt.int32
ALU = mybir.AluOpType
ACT = mybir.ActivationFunctionType
AX = mybir.AxisListType

P = 128
S = 256
T = S // P
D = 1024
KC = D // P
N = 512
IN_W = 9728
RH, RDK, RDV = 4, 128, 256
PATTERNS = ((128, 1), (512, 4), (2048, 16))
AG, AH, ADH = 3, 4, 128
BUCKETS, MAX_EXACT, MAX_DIST = 32, 16, 2048
E = 32
CAP = 64
ROUNDS = S // CAP
LIMIT, SWISH = 7.0, 1.702
EPS, GN_EPS, LN_EPS = 1e-6, 1e-5, 1e-5
NEG = -1.0e30
HEADS, DH = 12, 64
W_MIX, W_MEM, M_HEADS, N_MEM = HEADS * DH, 256, 4, 256
F2 = int(math.ceil(8 * D / 3 / 256) * 256)
FC2 = F2 // P
DEPTH_2 = 2
ALPHA = (2.0 * DEPTH_2) ** 0.25
SLOT = 2048
RING = 12
BANKS = 8
WIDE = 256
UNIT = SLOT // 2
BUFFERS = 4
TAB = 384

TABLES = {
    "common": (("ident", P), ("ones", P)),
    "mixer": (("anti", P), ("cos", T * 64), ("sin", T * 64), ("decay", 2 * RH * P)),
    "later": (("before", P), ("upto", P), ("causal", S), ("slots", ROUNDS * P)),
}
AT, TABLE_W = {}, {}
for _table, _cols in TABLES.items():
    _at = 0
    for _name, _width in _cols:
        AT[_name] = (_table, _at, _width)
        _at += _width
    TABLE_W[_table] = _at


def bucket_of(dist):
    ratio = np.log(np.maximum(dist, 1).astype(np.float32) / np.float32(MAX_EXACT)) / np.float32(math.log(MAX_DIST / MAX_EXACT))
    large = np.minimum(MAX_EXACT + (ratio * np.float32(BUCKETS - MAX_EXACT)).astype(np.int32), BUCKETS - 1)
    return np.where(dist < MAX_EXACT, dist, large)


def shape_constants():
    tables = {name: np.zeros((P, w), np.float32) for name, w in TABLE_W.items()}

    def put(name, value):
        table, a, w = AT[name]
        tables[table][:, a:a + w] = np.asarray(value, np.float32).reshape(P, w)

    i = np.arange(P)
    put("ident", np.eye(P))
    put("anti", np.eye(P)[::-1])
    put("before", i[:, None] < i[None, :])
    put("upto", i[:, None] <= i[None, :])
    put("ones", np.ones((P, P)))
    q, k = np.arange(P)[:, None] + P, np.arange(S)[None, :]
    put("causal", np.where(k <= q, 0.0, NEG))
    half = RDK // 2
    inv = np.float32(10000.0) ** (-np.arange(half, dtype=np.float32) / np.float32(half))
    pos = np.arange(S, dtype=np.float32).reshape(T, P).T
    ang = (pos[:, :, None] * inv[None, None, :]).astype(np.float32)
    put("cos", np.cos(ang))
    put("sin", np.sin(ang))
    log_g = np.log1p(-np.exp2(-5.0 - np.arange(RH)))
    diff = i[None, :] - i[:, None] + P * np.arange(2)[:, None, None]
    decay = np.where(diff[:, None] >= 0, np.exp(np.maximum(diff, 0)[:, None] * log_g[None, :, None, None]), 0.0)
    put("decay", decay.transpose(2, 0, 1, 3) * RDK ** -0.5)
    put("slots", np.broadcast_to(CAP * np.arange(ROUNDS)[:, None, None] + np.arange(CAP)[None, None, :], (P, ROUNDS, 2, CAP)))
    onehot = np.zeros((BUCKETS + 1, AG, TAB), np.float32)
    dist = S - 1 - np.arange(TAB)
    for g, (w, r) in enumerate(PATTERNS):
        ok = (dist >= 0) & (dist % r == 0) & (dist // r <= w // r)
        onehot[bucket_of(np.maximum(dist, 0)), g, np.arange(TAB)] = ok
        onehot[BUCKETS, g] = np.where(ok, 0.0, NEG)
    return tables, onehot


class Job:

    def __init__(self, name, by, slots, units):
        self.name, self.by, self.slots, self.units = name, by, slots, units
        self.index = self.bank = self.freed = self.before = self.hi = None
        self.apart = False


class Jobs:

    def __init__(self, banks):
        self.banks, self.turn = list(banks), 0
        self.list, self.by_name, self.counts, self.last_in = [], {}, {"act": 0, "dve": 0}, {}
        self.jobs = self.highs = self.parts = 0
        self.slots, self.units, self.released, self.raw_released = [], [], {}, {}

    def _slot(self, kind, src):
        q = len(self.slots)
        k, n = src.shape[1], src.shape[2]
        if kind == "raw":
            self.slots.append((kind, src, []))
            return q
        parts = 2 if kind == "wide" else -(-k * n // UNIT)
        new = list(range(len(self.units), len(self.units) + parts))
        for part in range(parts):
            chunks = KC if kind == "wide" else min(UNIT // n, k - part * (UNIT // n))
            self.units.append((q, part, chunks, n))
        self.slots.append((kind, src, new))
        return q

    def rows(self, w, col, n=N):
        per = SLOT // n
        total = w.shape[0] // P
        return [self._slot("rows", w[P * k:P * min(k + per, total), col:col + n].rearrange("(k p) n -> p k n", p=P)) for k in range(0, total, per)]

    def wide(self, w, col):
        return [self._slot("wide", w[:, col:col + WIDE].rearrange("(k p) n -> p k n", p=P))]

    def raw(self, src):
        return [self._slot("raw", src)]

    def add(self, name, by, slots=(), bank=None, high=False):
        job = Job(name, by, list(slots), [u for q in slots for u in self.slots[q][2]])
        job.index = self.jobs
        self.jobs += 1
        if bank is None:
            bank = self.banks[self.turn % len(self.banks)]
            self.turn += 1
        job.bank, job.before = bank, self.last_in.get(bank)
        self.last_in[bank] = job
        self.counts[by] += 1
        job.freed = self.counts[by]
        if high:
            self.highs += 1
            job.hi = self.highs
        self.list.append(job)
        self.by_name[name] = job
        self._release(job)
        return job

    def pair(self, name, by, slots, apart=False):
        for t in range(T):
            self.add(f"{name}t{t}", by, slots).apart = apart

    def piece(self, name, slots):
        job = Job(name, None, list(slots), [])
        self.list.append(job)
        self.parts += 1
        self.raw_released[slots[-1]] = ("part", self.parts)

    def _release(self, job):
        for u in job.units[:-1]:
            if u not in self.released:
                self.parts += 1
                self.released[u] = ("part", self.parts)
        if job.units:
            self.released[job.units[-1]] = ("full", job.index + 1)
        for q in job.slots:
            if self.slots[q][0] == "raw":
                if q == job.slots[-1]:
                    self.raw_released[q] = ("full", job.index + 1)
                else:
                    self.parts += 1
                    self.raw_released[q] = ("part", self.parts)

    def full(self, name):
        return self.by_name[name].index + 1

    def sequence(self):
        passed = 0
        head = [n for n, job in enumerate(self.list) if 0 in job.units][0]
        raw = [n for n, job in enumerate(self.list[:head]) if job.slots]
        start = raw[-1] if raw else head - 1
        for n, job in enumerate(self.list):
            if n == start + 1:
                yield from (("split", u) for u in range(min(BUFFERS, len(self.units))))
            before, after = job.units, []
            if job.apart:
                shared = len(job.units) - BUFFERS
                if job.name[-1] == "0":
                    before = job.units[:shared]
                else:
                    before, after = job.units[shared:-1], job.units[-1:]
            for part in (before, after):
                for u in part:
                    if u == passed:
                        passed += 1
                        if u + BUFFERS < len(self.units):
                            yield "split", u + BUFFERS
                if part is before:
                    yield "job", job


class Stream:

    def __init__(self, nc, sem, jobs, ring, ring_slots, high, low):
        self.nc, self.jobs, self.ring, self.ring_slots, self.high, self.low = nc, jobs, ring, ring_slots, high, low
        self.full, self.part = sem("full"), sem("part_done")
        self.freed = {"act": sem("freed_by_act"), "dve": sem("freed_by_dve")}
        self.slot_here = [sem(f"slot_here{k}") for k in range(ring_slots)]
        self.hi_ready, self.lo_ready = sem("hi_ready"), sem("lo_ready")

    def wait_tensor(self, eng, release):
        which, n = release
        eng.wait_ge(self.full if which == "full" else self.part, n)

    def wait_freed(self, eng, name):
        job = self.jobs.by_name[name]
        eng.wait_ge(self.freed[job.by], job.freed)

    def wait_here(self, eng, q):
        eng.wait_ge(self.slot_here[q % self.ring_slots], 16 * (q // self.ring_slots + 1))

    def load(self, sp, q):
        kind, src, _ = self.jobs.slots[q]
        if q >= self.ring_slots:
            old = q - self.ring_slots
            if self.jobs.slots[old][0] == "raw":
                self.wait_tensor(sp, self.jobs.raw_released[old])
            else:
                sp.wait_ge(self.lo_ready, self.jobs.slots[old][2][-1] + 1)
        k, n = src.shape[1], src.shape[2]
        at = (q % self.ring_slots) * SLOT
        sp.dma_start(self.ring[:, at:at + k * n].rearrange("p (k n) -> p k n", n=n), src).then_inc(self.slot_here[q % self.ring_slots], 16)

    def views(self, u):
        q, part, chunks, n = self.jobs.units[u]
        at = (q % self.ring_slots) * SLOT
        if self.jobs.slots[q][0] == "wide":
            raw = self.ring[:, at:at + SLOT].rearrange("p (k n) -> p k n", k=KC)[:, :, P * part:P * part + P]
            return raw, *(b[:, u % BUFFERS, :].rearrange("p (k n) -> p k n", k=KC) for b in (self.high, self.low))
        raw = self.ring[:, at + UNIT * part:at + UNIT * part + chunks * n]
        return raw, self.high[:, u % BUFFERS, 0:chunks * n], self.low[:, u % BUFFERS, 0:chunks * n]

    def split_high(self, act, u):
        raw, hi, _ = self.views(u)
        self.wait_here(act, self.jobs.units[u][0])
        if u >= BUFFERS:
            self.wait_tensor(act, self.jobs.released[u - BUFFERS])
        self.nc.scalar.copy(hi, raw).then_inc(self.hi_ready, 1)

    def split_low(self, dve, u):
        raw, hi, lo = self.views(u)
        dve.wait_ge(self.hi_ready, u + 1)
        self.nc.vector.tensor_tensor(lo, raw, hi.bitcast(FP32), ALU.subtract).then_inc(self.lo_ready, 1)

    def start(self, pe, job):
        if job.before is not None:
            pe.wait_ge(self.freed[job.before.by], job.before.freed)

    def natural(self, pe, jobs, outs, xh, xl, ready=None):
        units = jobs[0].units
        total = sum(self.jobs.units[u][2] for u in units)
        shared = len(units) - BUFFERS if jobs[0].apart else len(units)
        passes = [(u, range(T), True) for u in units[:shared]]
        for t in range(T):
            passes += [(u, (t,), t == T - 1) for u in units[shared:]]
        per = self.jobs.units[units[0]][2]
        for u, tiles, final in passes:
            _, _, chunks, n = self.jobs.units[u]
            pe.wait_ge(self.lo_ready, u + 1)
            if ready is not None:
                ready(u - units[0])
            k = per * (u - units[0])
            for c in range(chunks):
                hi, lo = (b[:, u % BUFFERS, n * c:n * c + n] for b in (self.high, self.low))
                for t in tiles:
                    s = slice(P * t, P * t + P)
                    self.nc.tensor.matmul(outs[t], xh[:, k, s], hi, start=k == 0, stop=False)
                    self.nc.tensor.matmul(outs[t], xh[:, k, s], lo, start=False, stop=False)
                    last = self.nc.tensor.matmul(outs[t], xl[:, k, s], hi, start=False, stop=k == total - 1)
                    if k == total - 1:
                        last.then_inc(self.full, 1)
                k += 1
            if final and u != units[-1]:
                last.then_inc(self.part, 1)

    def transposed(self, pe, job, bank, xh, xl):
        for a, u in enumerate(job.units):
            pe.wait_ge(self.lo_ready, u + 1)
            for k in range(KC):
                out = bank[:, S * a:S * a + S]
                hi, lo = (b[:, u % BUFFERS, P * k:P * k + P] for b in (self.high, self.low))
                self.nc.tensor.matmul(out, hi, xh[:, k, :], start=k == 0, stop=False)
                self.nc.tensor.matmul(out, hi, xl[:, k, :], start=False, stop=False)
                last = self.nc.tensor.matmul(out, lo, xh[:, k, :], start=False, stop=k == KC - 1)
            last.then_inc(self.full if u == job.units[-1] else self.part, 1)


class Chain:

    def __init__(self, eng, sem):
        self.eng, self.sem, self.n = eng, sem, 0

    def __call__(self, ins):
        self.n += 1
        ins.then_inc(self.sem, 1)
        self.eng.wait_ge(self.sem, self.n)

    def mark(self, ins):
        self.n += 1
        ins.then_inc(self.sem, 1)

    def sync(self):
        self.eng.wait_ge(self.sem, self.n)


def free(tile, at, *shape):
    w = int(np.prod(shape))
    v = tile[:, at:at + w]
    if len(shape) == 1:
        return v
    names = "abcd"[:len(shape)]
    return v.rearrange("p (%s) -> p %s" % (" ".join(names), " ".join(names)), **{n: s for n, s in zip(names[1:], shape[1:])})


def const(M, name, *shape):
    table, a, w = AT[name]
    return free(M[table], a, *(shape or (w,)))


def mixer(nc, M, A, scratch):
    x_sb, bank, small = M["x"], M["bank"], M["small"]
    ctx = ExitStack()
    RING_MIX = 4
    base = M["base"]
    arena = ctx.enter_context(nc.sbuf_tensor("mixer_arena", [P, 18944], FP32))
    M = dict(M, mixer=ctx.enter_context(nc.sbuf_tensor("mixer_consts", [P, TABLE_W["mixer"]], FP32)))
    ring = ctx.enter_context(nc.sbuf_tensor("mixer_ring", [P, RING_MIX * SLOT], FP32))
    high = ctx.enter_context(nc.sbuf_tensor("mixer_w_hi", [P, BUFFERS, UNIT], F32R))
    low = ctx.enter_context(nc.sbuf_tensor("mixer_w_lo", [P, BUFFERS, UNIT], F32R))
    xh = ctx.enter_context(nc.sbuf_tensor("mixer_x_hi", [P, 2 * KC, S], F32R))
    xl = ctx.enter_context(nc.sbuf_tensor("mixer_x_lo", [P, 2 * KC, S], F32R))

    rows_mod = free(base, 0, 4, D)
    aqT = free(base, 0, AG * AH, S)
    rot = free(arena, 0, T, 2, RH, RDK)
    hnat = free(arena, 0, T, D)
    ynat = free(arena, 0, T, D)
    m1 = free(arena, 0, T, D)
    qkT = free(arena, 2048, 2, RH, S)
    probs = free(arena, 2048, 2, AG, S)
    onehot = arena[0:BUCKETS + 1, 2048:2048 + AG * TAB].rearrange("p (g n) -> p g n", g=AG)
    rv = free(arena, 4096, T, D)
    sig = free(arena, 4096, T, D)
    rg = free(arena, 6144, T, D)
    akT = free(arena, 8192, AG * AH, S)
    g_ffn_row = free(arena, 8192, D)
    gs, sh, g_row = free(arena, 11264, D), free(arena, 12288, D), free(arena, 13312, D)
    av = free(arena, 11264, T, AG * AH * ADH)
    probsT = free(arena, 14336, 2, 2 * AG, P)
    tab = arena[0:AH, 14336:14336 + AG * TAB].rearrange("p (g n) -> p g n", g=AG)
    sT = free(arena, 14336, 2, 2, P)
    rtmp = free(arena, 14848, 2, RH, 64)
    hankel = free(arena, 15872, AG, AH, S)
    mod4 = free(base, 3072, 2, N)
    sumsq, rstd = small[:, 0:2], small[:, 2:4]
    cs, bias_rel = small[:, 8:16], small[0:BUCKETS + 1, 16:28]
    stats, mv = free(small, 32, RH, 6), free(small, 64, RH, 2)
    negmax, mx2, lsum, rsum = small[:, 80:82], free(small, 84, 2, 2), free(small, 88, 2, 2), small[:, 92:94]
    csb = free(small, 128, KC, 32)
    c8, b12 = arena[0:KC, 4096:4096 + P], M["b12"]
    ident = const(M, "ident")

    jobs = Jobs(range(BANKS - 1))
    w_in = A["w_in"][0]

    def ada_slot(g, k):
        return jobs.raw(A["w_ada"][0, k * P:(k + 1) * P, SLOT * g:SLOT * (g + 1)].rearrange("p (k n) -> p k n", k=4))

    ada_left = [(g, k) for g in (1, 2) for k in range(KC)]

    def some_ada():
        if ada_left:
            g, k = ada_left.pop(0)
            if k < KC - 1:
                jobs.piece(f"ada{g}.{k}", ada_slot(g, k))
            else:
                jobs.add(f"ada{g}", "dve", ada_slot(g, k), bank=BANKS - 1)

    jobs.add("cT", "act")
    for g in range(AG):
        jobs.add(f"tab{g}", "act")
    for k in range(KC - 1):
        jobs.piece(f"ada0.{k}", ada_slot(0, k))
    jobs.add("ada0", "dve", ada_slot(0, KC - 1), bank=BANKS - 1)
    for n in range(4):
        jobs.add(f"mod{n}", "act" if n < 2 else "dve")
    for t in range(T):
        for half in range(2):
            jobs.add(f"hT{t}{half}", "dve", high=True)
    for name, col in (("rq", 0), ("rk", 512), ("rv0", 1024), ("rv1", 1536)):
        jobs.pair(name, "dve" if name in ("rq", "rk") else "act", jobs.rows(w_in, col))
    for n in range(2):
        for t in range(T):
            jobs.add(f"rT{n}{t}", "act")
    for n in range(2):
        jobs.pair(f"rg{n}", "act", jobs.rows(w_in, 2048 + N * n))
    units = [(h, t) for h in range(RH) for t in range(T)]
    fill = []
    for u in range(len(units) + 1):
        fill.append(([f"rs{u}"] if u < len(units) else []) + ([f"ry{u - 1}"] if u else []))
    fill += [[], []]
    for what, col in (("aq", 3072), ("ak", 4608)):
        for n in range(AG * AH // 2):
            jobs.add(f"{what}{n}", "act", jobs.wide(w_in, col + WIDE * n))
            for name in (fill.pop(0) if fill else []):
                jobs.add(name, "dve")
            some_ada()
    for g in range(AG - 1):
        jobs.pair(f"av{g}", "act", jobs.rows(w_in, 6144 + N * g))
        if g == 0:
            for n in range(4):
                jobs.add(f"retT{n}", "dve", high=True)
        some_ada()
    filler = [(f"av{AG - 1}", "act", w_in, 6144 + N * (AG - 1))]
    filler += [(f"{what}{half}", by, w, col + N * half)
              for what, by, w, col in (("ro", "act", A["w_ret_o"][0], 0), ("ga", "act", w_in, 7680), ("gb", "act", w_in, 8704)) for half in range(2)]
    for u in range(len(units) + 1):
        if u:
            for n in range(1 + units[u - 1][1]):
                jobs.add(f"pT{u - 1}{n}", "act")
        if u < len(units):
            jobs.add(f"sa{u}", "act")
            jobs.add(f"sb{u}", "act")
        if u > 1:
            jobs.add(f"ao{u - 1}", "dve", high=True)
        if filler:
            for _ in range(2 if u == 1 else 1):
                name, by, w, col = filler.pop(0)
                jobs.pair(name, by, jobs.rows(w, col))
            if u == 1:
                jobs.add("ao0", "dve", high=True)
        elif u == len(units) - 1:
            for n in range(4, 8):
                jobs.add(f"mod{n}", "act")
        some_ada()
    assert not filler and not ada_left
    for half in range(2):
        jobs.pair(f"to{half}", "dve", jobs.rows(A["w_att_o"][0], N * half))
    for n in range(8, 12):
        jobs.add(f"mod{n}", "dve" if n in (8, 9) else "act")
    for t in range(T):
        for half in range(2):
            jobs.add(f"mT{t}{half}", "dve", high=True)
    for half in range(2):
        jobs.pair(f"wo{half}", "dve", jobs.rows(A["w_o"][0], N * half))

    with ctx:
        def sem(name):
            return ctx.enter_context(nc.semaphore("mix_" + name))

        stream = Stream(nc, sem, jobs, ring, RING_MIX, high, low)
        full, freed_by_act, freed_by_dve = stream.full, stream.freed["act"], stream.freed["dve"]
        wait_freed, xh_ready, ga_applied = stream.wait_freed, sem("xh_ready"), sem("ga_applied")
        const_here, x_here, row_here, tiny_here, rel_here = sem("const_here"), sem("x_here"), sem("row_here"), sem("tiny_here"), sem("rel_here")
        ffn_row_here = sem("ffn_row_here")
        rel_ready, table_out, bias_here = sem("rel_ready"), sem("table_out"), sem("bias_here")
        dve_step, act_step = sem("dve_step"), sem("act_step")
        squares_ready, mean_ready, root_ready = sem("squares_ready"), sem("mean_ready"), sem("root_ready")
        cs_ready, csb_ready, h_ready, rot_ready = sem("cs_ready"), sem("csb_ready"), sem("h_ready"), sem("rot_ready")
        var_ready, ret_root_ready, ret_ready = sem("var_ready"), sem("ret_root_ready"), sem("ret_ready")
        max_ready, probs_ready, merged_ready, x_ready = sem("max_ready"), sem("probs_ready"), sem("merged_ready"), sem("x_ready")
        block = ctx.enter_context(nc.Block())

        def high_places(job, b, parts=None):
            parts = xh if parts is None else parts
            name = job.name
            if name.startswith("ao"):
                h, t = units[int(name[2:])]
                return parts[:, KC + h, P * t:P * t + P], b[:, 0:P]
            t, half = (int(name[4]) // 2, int(name[4]) % 2) if name.startswith("retT") else (int(name[2]), int(name[3]))
            at = 4 * half + (KC if name.startswith("retT") else 0)
            return parts[:, at:at + 4, P * t:P * t + P], b.rearrange("p (k s) -> p k s", k=4)

        @block.sync
        def _(sp):
            sp.dma_start(c8, A["c"][0].rearrange("(k p) -> k p", p=P)).then_inc(tiny_here, 16)
            sp.dma_start(M["b12"][:, :], A["b_ada"][0].rearrange("(k n) -> k n", n=N)).then_inc(tiny_here, 16)
            for table in ("common", "mixer"):
                sp.dma_start(M[table][:, :], A["table_" + table]).then_inc(const_here, 16)
            sp.dma_start(x_sb[:, :, :], A["x"][0].rearrange("(t p) d -> p t d", p=P)).then_inc(x_here, 16)
            sp.dma_start(g_row.unsqueeze(1), A["g_mix"][0:1, :].partition_broadcast(P)).then_inc(row_here, 16)
            for q in range(len(jobs.slots)):
                stream.load(sp, q)

        @block.gpsimd
        def _(pool):
            pool.memset(bias_rel[BUCKETS:BUCKETS + 1, :], 1.0).then_inc(rel_ready, 1)
            pool.dma_start(bias_rel[0:BUCKETS, :], A["rel_bias"]).then_inc(rel_here, 16)
            pool.dma_start(onehot, A["onehot"]).then_inc(rel_here, 16)
            wait_freed(pool, "tab2")
            pool.dma_start(scratch.rearrange("(g h) n -> h g n", g=AG), tab).then_inc(table_out, 16)
            pool.wait_ge(table_out, 16)
            for g in range(AG):
                shifted = bass.AP(tensor=scratch.tensor, offset=g * AH * TAB, ap=[[1, P], [TAB, AH], [1, S]])
                pool.dma_start(hankel[:, g], shifted).then_inc(bias_here, 16)
            pool.wait_ge(full, jobs.full("sb7"))
            pool.dma_start(g_ffn_row.unsqueeze(1), A["g_ffn"][0:1, :].partition_broadcast(P)).then_inc(ffn_row_here, 16)
            pool.wait_ge(ffn_row_here, 16)

        @block.scalar
        def _(act):
            chain = Chain(act, act_step)

            def rms_roots(src):
                for t in range(T):
                    nc.scalar.activation(hnat[:, t, :], src[:, t, :], ACT.Square, accum_out=sumsq[:, t:t + 1]).then_inc(squares_ready, 1)
                act.wait_ge(mean_ready, 1)
                nc.scalar.activation(rstd, rstd, ACT.Sqrt).then_inc(root_ready, 1)

            for what, job in jobs.sequence():
                if what == "split":
                    stream.split_high(act, job)
                    continue
                name = job.name
                if job.index is None:
                    continue
                b = bank[job.bank]
                if job.hi:
                    act.wait_ge(full, job.index + 1)
                    dst, src = high_places(job, b)
                    nc.scalar.copy(dst, src).then_inc(xh_ready, 1)
                    continue
                if job.by != "act":
                    if name == "ry7":
                        act.wait_ge(var_ready, 1)
                        nc.scalar.activation(M["var8"], M["var8"], ACT.Sqrt).then_inc(ret_root_ready, 1)
                    continue
                if name == "tab0":
                    act.wait_ge(x_here, 16)
                    rms_roots(x_sb)
                act.wait_ge(full, job.index + 1)
                last = None
                if name == "cT":
                    last = nc.scalar.activation(cs, b[:, 0:KC], ACT.Silu)
                elif name.startswith("tab"):
                    last = nc.scalar.copy(tab[:, int(name[3:]), :], b[0:AH, 0:TAB])
                elif name.startswith("mod"):
                    n = int(name[3:])
                    if n < 4:
                        dst = sh[:, N * n:N * n + N]
                    else:
                        dst = rows_mod[:, {4: 0, 6: 1, 10: 3}[n - n % 2], N * (n % 2):N * (n % 2) + N]
                    last = nc.scalar.copy(dst, b)
                elif name.startswith("rv"):
                    n, t = int(name[2]), int(name[4])
                    last = nc.scalar.copy(rv[:, t, N * n:N * n + N], b)
                elif name.startswith("rT"):
                    n, t = int(name[2]), int(name[3])
                    last = nc.scalar.copy(qkT[:, n, :, P * t:P * t + P], b.rearrange("p (h s) -> p h s", h=RH))
                elif name.startswith("rg"):
                    n, t = int(name[2]), int(name[4])
                    last = nc.scalar.activation(rg[:, t, N * n:N * n + N], b, ACT.Silu)
                elif name.startswith("aq"):
                    n = int(name[2:])
                    last = nc.scalar.mul(aqT[:, 2 * n:2 * n + 2, :], b.rearrange("p (a s) -> p a s", a=2), ADH ** -0.5)
                elif name.startswith("ak"):
                    n = int(name[2:])
                    last = nc.scalar.copy(akT[:, 2 * n:2 * n + 2, :], b.rearrange("p (a s) -> p a s", a=2))
                elif name.startswith("av"):
                    g, t = int(name[2]), int(name[4])
                    last = nc.scalar.copy(av[:, t, N * g:N * g + N], b)
                elif name.startswith("ro"):
                    half, t = int(name[2]), int(name[4])
                    last = nc.scalar.copy(m1[:, t, N * half:N * half + N], b)
                elif name[:2] in ("ga", "gb"):
                    half, t = int(name[2]), int(name[4])
                    if name == "gb0t0":
                        act.wait_ge(ga_applied, 2 * T)
                    last = nc.scalar.activation(sig[:, t, N * half:N * half + N], b, ACT.Sigmoid)
                elif name[:2] in ("sa", "sb"):
                    u = int(name[2:])
                    h, t = units[u]
                    w, part = P * (t + 1), "ab".index(name[1])
                    act.wait_ge(max_ready, u + 1)
                    groups = 1 if part else 2
                    src = b.rearrange("p (g k) -> p g k", k=S)[:, 0:groups, 0:w]
                    last = nc.scalar.activation(probs[:, u % 2, 2 * part:2 * part + groups, 0:w], src, ACT.Exp,
                                                bias=negmax[:, u % 2:u % 2 + 1], accum_out=lsum[:, u % 2, part:part + 1])
                elif name.startswith("pT"):
                    u, n = int(name[2:-1]), int(name[-1])
                    last = nc.scalar.copy(probsT[:, u % 2, AG * n:AG * n + AG, :], b[:, 0:AG * P].rearrange("p (g s) -> p g s", g=AG))
                last.then_inc(freed_by_act, 1)

        @block.vector
        def _(dve):
            step = Chain(dve, dve_step)
            wait_freed(dve, "cT")
            nc.vector.tensor_copy(csb, cs.unsqueeze(2).to_broadcast([P, KC, 32])).then_inc(csb_ready, 1)
            dve.wait_ge(squares_ready, T)
            nc.vector.tensor_scalar(rstd, sumsq, 1.0 / D, EPS, ALU.mult, ALU.add).then_inc(mean_ready, 1)
            dve.wait_ge(root_ready, 1)
            step(nc.vector.reciprocal(rstd, rstd))
            dve.wait_ge(x_here, 16)
            for t in range(T):
                step.mark(nc.vector.tensor_scalar(hnat[:, t, :], x_sb[:, t, :], rstd[:, t:t + 1], None, ALU.mult))
            step.sync()
            dve.wait_ge(const_here, 32)
            cos, sin = const(M, "cos", T, 64), const(M, "sin", T, 64)
            decay = const(M, "decay", 2, RH, P)

            def divide(u):
                w = P * (units[u][1] + 1)
                wait_freed(dve, f"sb{u}")
                step(nc.vector.tensor_tensor(rsum[:, u % 2:u % 2 + 1], lsum[:, u % 2, 0:1], lsum[:, u % 2, 1:2], ALU.add))
                step(nc.vector.reciprocal(rsum[:, u % 2:u % 2 + 1], rsum[:, u % 2:u % 2 + 1]))
                pr = probs[:, u % 2, :, 0:w]
                nc.vector.tensor_scalar(pr, pr, rsum[:, u % 2:u % 2 + 1], None, ALU.mult).then_inc(probs_ready, 1)

            for what, job in jobs.sequence():
                if what == "split":
                    stream.split_low(dve, job)
                    continue
                name = job.name
                if job.index is None:
                    continue
                b = bank[job.bank]
                if job.hi:
                    dve.wait_ge(full, job.index + 1)
                    dve.wait_ge(xh_ready, job.hi)
                    dst, src = high_places(job, b, xl)
                    nc.vector.tensor_tensor(dst, src, high_places(job, b)[0].bitcast(FP32), ALU.subtract).then_inc(freed_by_dve, 1)
                    if name[:2] == "ao" and 1 < int(name[2:]) + 1 < len(units):
                        divide(int(name[2:]) + 1)
                    continue
                if job.by != "dve":
                    if name[:2] == "ga":
                        half, t = int(name[2]), int(name[4])
                        cols = slice(N * half, N * half + N)
                        wait_freed(dve, f"ro{half}t{t}")
                        wait_freed(dve, name)
                        nc.vector.tensor_tensor(m1[:, t, cols], m1[:, t, cols], sig[:, t, cols], ALU.mult).then_inc(ga_applied, 1)
                    if name[:2] == "sb":
                        u = int(name[2:])
                        w = P * (units[u][1] + 1)
                        ba = bank[jobs.by_name[f"sa{u}"].bank].rearrange("p (g k) -> p g k", k=S)[:, :, 0:w]
                        dve.wait_ge(full, jobs.full(name))
                        step.mark(nc.vector.tensor_reduce(mx2[:, u % 2, 0:1], ba, AX.XY, ALU.max))
                        step(nc.vector.tensor_reduce(mx2[:, u % 2, 1:2], b[:, 0:w], AX.X, ALU.max))
                        nc.vector.tensor_reduce(negmax[:, u % 2:u % 2 + 1], mx2[:, u % 2, :], AX.X, ALU.max, negate=True).then_inc(max_ready, 1)
                        if u < 2:
                            divide(u)
                    continue
                if name.startswith("ada"):
                    dve.wait_ge(full, job.index + 1)
                    nc.vector.tensor_copy(mod4[:, int(name[3:]) // 2, :], b).then_inc(freed_by_dve, 1)
                    continue
                if name.startswith("mod"):
                    n = int(name[3:])
                    dve.wait_ge(full, job.index + 1)
                    half = N * (n % 2)
                    if n < 4:
                        dve.wait_ge(row_here, 16)
                        dst, row = gs, g_row
                    else:
                        dve.wait_ge(ffn_row_here, 16)
                        dst, row = rows_mod[:, 2, :], g_ffn_row
                    nc.vector.scalar_tensor_tensor(dst[:, half:half + N], b, 1.0, row[:, half:half + N], ALU.add, ALU.mult).then_inc(freed_by_dve, 1)
                    if n == 3:
                        dve.wait_ge(freed_by_dve, job.freed)
                        wait_freed(dve, "mod1")
                        for t in range(T):
                            step(nc.vector.tensor_tensor(hnat[:, t, :], hnat[:, t, :], gs, ALU.mult))
                            nc.vector.tensor_tensor(hnat[:, t, :], hnat[:, t, :], sh, ALU.add).then_inc(h_ready, 1)
                    continue
                if name[:2] in ("rq", "rk"):
                    i, t = "qk".index(name[1]), int(name[3])
                    dve.wait_ge(full, job.index + 1)
                    if T * i + t:
                        dve.wait_ge(rot_ready, T * i + t)
                    else:
                        dve.wait_ge(table_out, 16)
                    v = b.rearrange("p (h c) -> p h c", h=RH)
                    c1 = cos[:, t, :].unsqueeze(1).to_broadcast([P, RH, 64])
                    s1 = sin[:, t, :].unsqueeze(1).to_broadcast([P, RH, 64])
                    lo, hi = rot[:, t, i, :, 0:64], rot[:, t, i, :, 64:128]
                    step.mark(nc.vector.tensor_tensor(lo, v[:, :, 0:64], c1, ALU.mult))
                    step.mark(nc.vector.tensor_tensor(hi, v[:, :, 0:64], s1, ALU.mult))
                    step.mark(nc.vector.tensor_tensor(rtmp[:, 0], v[:, :, 64:128], s1, ALU.mult))
                    nc.vector.tensor_tensor(rtmp[:, 1], v[:, :, 64:128], c1, ALU.mult).then_inc(freed_by_dve, 1)
                    step.sync()
                    dve.wait_ge(freed_by_dve, job.freed)
                    step.mark(nc.vector.tensor_tensor(lo, lo, rtmp[:, 0], ALU.subtract))
                    nc.vector.tensor_tensor(hi, hi, rtmp[:, 1], ALU.add).then_inc(rot_ready, 1)
                    continue
                if name.startswith("rs"):
                    u = int(name[2:])
                    h, t = units[u]
                    dve.wait_ge(full, job.index + 1)
                    src = b[:, 0:P * (t + 1)].rearrange("p (j s) -> p j s", j=t + 1)
                    nc.vector.tensor_tensor(sT[:, u % 2, 0:t + 1, :], src, decay[:, 0:t + 1, h, :], ALU.mult).then_inc(freed_by_dve, 1)
                    continue
                if name.startswith("ry"):
                    u = int(name[2:])
                    h, t = units[u]
                    dve.wait_ge(full, job.index + 1)
                    step.mark(nc.vector.bn_stats(stats[:, u % RH, :], b[:, 0:RDV]))
                    step.sync()
                    step.mark(nc.vector.bn_aggr(M["mv8"][:, u, :], stats[:, u % RH, :]))
                    nc.vector.tensor_copy(ynat[:, t, RDV * h:RDV * h + RDV], b[:, 0:RDV]).then_inc(freed_by_dve, 1)
                    if u == 7:
                        step.sync()
                        dve.wait_ge(freed_by_dve, job.freed)
                        nc.vector.tensor_scalar(M["var8"], M["mv8"][:, :, 1], GN_EPS, None, ALU.add).then_inc(var_ready, 1)
                        dve.wait_ge(ret_root_ready, 1)
                        step(nc.vector.reciprocal(M["var8"], M["var8"]))
                        wait_freed(dve, "rg1t1")
                        for v, (h, t) in enumerate(units):
                            y = ynat[:, t, RDV * h:RDV * h + RDV]
                            step.mark(nc.vector.tensor_scalar(y, y, M["mv8"][:, v, 0:1], M["var8"][:, v:v + 1], ALU.subtract, ALU.mult))
                        step.sync()
                        for t in range(T):
                            nc.vector.tensor_tensor(rg[:, t, :], rg[:, t, :], ynat[:, t, :], ALU.mult).then_inc(ret_ready, 1)
                    continue
                half, t = int(name[2]), int(name[4])
                cols = slice(N * half, N * half + N)
                dve.wait_ge(full, job.index + 1)
                if name.startswith("to"):
                    wait_freed(dve, f"gb{half}t{t}")
                    nc.vector.tensor_tensor(sig[:, t, cols], sig[:, t, cols], b, ALU.mult).then_inc(freed_by_dve, 1)
                    dve.wait_ge(freed_by_dve, job.freed)
                    dve.wait_ge(ga_applied, 2 * T)
                    nc.vector.tensor_tensor(m1[:, t, cols], m1[:, t, cols], sig[:, t, cols], ALU.add).then_inc(merged_ready, 1)
                elif name.startswith("wo"):
                    wait_freed(dve, "mod5")
                    dve.wait_ge(merged_ready, 2 * T)
                    nc.vector.tensor_tensor(sig[:, t, cols], b, rows_mod[:, 0, cols], ALU.mult).then_inc(freed_by_dve, 1)
                    dve.wait_ge(freed_by_dve, job.freed)
                    nc.vector.tensor_tensor(x_sb[:, t, cols], x_sb[:, t, cols], sig[:, t, cols], ALU.add).then_inc(x_ready, 1)
            dve.wait_ge(x_ready, 2 * T)

        @block.tensor
        def _(pe):
            ones, anti = const(M, "ones"), const(M, "anti")
            pe.wait_ge(const_here, 32)
            pe.wait_ge(tiny_here, 32)

            def ada_products(b, q, k):
                stream.wait_here(pe, q)
                at = (q % RING_MIX) * SLOT
                for j in range(4):
                    last = nc.tensor.matmul(b[32 * j:32 * j + 32, :], csb[:, k, :], ring[:, at + N * j:at + N * j + N], start=k == 0, stop=False)
                return last

            for job in jobs.list:
                name = job.name
                if job.index is None:
                    g, k = int(name[3]), int(name[5])
                    if k == 0:
                        if g == 0:
                            pe.wait_ge(csb_ready, 1)
                        stream.start(pe, jobs.by_name[f"ada{g}"])
                    ada_products(bank[BANKS - 1], job.slots[0], k).then_inc(stream.part, 1)
                    continue
                b = bank[job.bank]
                if len(job.units) and name[-2:] == "t1":
                    continue
                stream.start(pe, job)
                if name == "cT":
                    last = nc.tensor.transpose(b[:, 0:KC], c8[:, :], ident[0:KC, 0:KC])
                elif name.startswith("tab"):
                    g = int(name[3:])
                    if g == 0:
                        pe.wait_ge(rel_ready, 1)
                        pe.wait_ge(rel_here, 32)
                    last = nc.tensor.matmul(b[0:AH, 0:TAB], bias_rel[:, AH * g:AH * g + AH], onehot[:, g, :], start=True, stop=True)
                elif name.startswith("ada"):
                    g = int(name[3:])
                    ada_products(b, job.slots[0], KC - 1)
                    for j in range(4):
                        pick = ident[0:12, 4 * g + j:4 * g + j + 1].to_broadcast([12, 32])
                        last = nc.tensor.matmul(b[32 * j:32 * j + 32, :], pick, b12[:, :], start=False, stop=True)
                elif name.startswith("mod"):
                    n = int(name[3:])
                    wait_freed(pe, f"ada{n // 4}")
                    r = 32 * (n % 4)
                    last = nc.tensor.matmul(b, ones[r:r + 1, :], mod4[r:r + 1, n // 8, :], start=True, stop=True)
                elif name.startswith("hT") or name.startswith("mT"):
                    t, half = int(name[2]), int(name[3])
                    if name[0] == "h":
                        pe.wait_ge(h_ready, t + 1)
                    else:
                        pe.wait_ge(merged_ready, 2 * T)
                    src = hnat if name[0] == "h" else m1
                    for k in range(4):
                        last = nc.tensor.transpose(b[:, P * k:P * k + P], src[:, t, N * half + P * k:N * half + P * k + P], ident)
                elif name.startswith("rT"):
                    i, t = int(name[2]), int(name[3])
                    pe.wait_ge(rot_ready, T * i + t + 1)
                    for h in range(RH):
                        last = nc.tensor.transpose(b[:, P * h:P * h + P], rot[:, t, i, h, :], ident)
                elif name.startswith("retT"):
                    n = int(name[4])
                    pe.wait_ge(ret_ready, n // 2 + 1)
                    for k in range(4):
                        at = N * (n % 2) + P * k
                        last = nc.tensor.transpose(b[:, P * k:P * k + P], rg[:, n // 2, at:at + P], ident)
                elif name.startswith("rs"):
                    h, t = units[int(name[2:])]
                    wait_freed(pe, "rT11")
                    for back in range(t + 1):
                        j = t - back
                        last = nc.tensor.matmul(b[:, P * back:P * back + P], qkT[:, 1, h, P * j:P * j + P], qkT[:, 0, h, P * t:P * t + P], start=True, stop=True)
                elif name.startswith("ry"):
                    u = int(name[2:])
                    h, t = units[u]
                    wait_freed(pe, "rv1t1")
                    wait_freed(pe, f"rs{u}")
                    for back in range(t + 1):
                        last = nc.tensor.matmul(b[:, 0:RDV], sT[:, u % 2, back, :], rv[:, t - back, RDV * h:RDV * h + RDV], start=back == 0, stop=back == t)
                elif name[:2] in ("aq", "ak"):
                    stream.transposed(pe, job, b, xh, xl)
                    continue
                elif name[:2] in ("sa", "sb"):
                    u = int(name[2:])
                    h, t = units[u]
                    w = P * (t + 1)
                    if u == 0:
                        pe.wait_ge(bias_here, 16 * AG)
                    wait_freed(pe, f"ak{(AG * AH) // 2 - 1}")
                    for g in ((0, 1) if name[1] == "a" else (2,)):
                        out = b[:, S * (g % 2):S * (g % 2) + w]
                        nc.tensor.matmul(out, aqT[:, AH * g + h, P * t:P * t + P], akT[:, AH * g + h, 0:w], start=True, stop=False)
                        last = nc.tensor.matmul(out, anti, hankel[:, g, h, S - w:S], start=False, stop=True)
                elif name.startswith("pT"):
                    u, n = int(name[2:-1]), int(name[-1])
                    pe.wait_ge(probs_ready, u + 1)
                    for g in range(AG):
                        last = nc.tensor.transpose(b[:, P * g:P * g + P], probs[:, u % 2, g, P * n:P * n + P], ident)
                elif name.startswith("ao"):
                    u = int(name[2:])
                    h, t = units[u]
                    wait_freed(pe, "av2t1")
                    wait_freed(pe, f"pT{u}{t}")
                    for n in range(t + 1):
                        for g in range(AG):
                            at = (AH * g + h) * ADH
                            last = nc.tensor.matmul(b[:, 0:P], av[:, n, at:at + ADH], probsT[:, u % 2, AG * n + g, :],
                                                    start=n + g == 0, stop=n == t and g == AG - 1)
                else:
                    other = jobs.by_name[name[:-1] + "1"]
                    stream.start(pe, other)
                    at = KC if name[:2] in ("ro", "to") else 0
                    if name == "rqt0":
                        wait_freed(pe, "hT11")
                    elif name.startswith("ro"):
                        wait_freed(pe, "retT3")
                    elif name.startswith("to"):
                        wait_freed(pe, "ao7")
                    elif name.startswith("wo"):
                        wait_freed(pe, "mT11")
                    stream.natural(pe, (job, other), (b, bank[other.bank]), xh[:, at:at + KC, :], xl[:, at:at + KC, :])
                    continue
                last.then_inc(full, 1)


def experts(nc, M, A):
    x_sb, psum, bank, small = M["x"], M["psum"], M["bank"], M["small"]
    ctx = ExitStack()
    ring = ctx.enter_context(nc.sbuf_tensor("expert_ring", [P, RING * SLOT], FP32))
    arena = ctx.enter_context(nc.sbuf_tensor("expert_arena", [P, 12800], FP32))
    actT = ctx.enter_context(nc.sbuf_tensor("expert_hT", [P, KC, S], FP32))
    hn = free(arena, 0, T, D)
    b1 = arena[0:E, 2048:4096]
    b2 = arena[0:E, 4096:5120]
    wr = free(arena, 5120, KC, E)
    br = free(arena, 5376, E)
    rows_mod = free(M["base"], 0, 4, D)
    pick = free(arena, 7168, T, CAP)
    gated = free(arena, 7296, T, P)
    xg = free(arena, 7552, KC, CAP)
    glu, sig, lin, act_out = (free(arena, 8064 + N * i, N) for i in range(4))
    aT = free(arena, 10112, 4, P)
    gatedT = free(arena, 10624, T, P)
    y_sb = free(arena, 10880, N)
    zeros = free(arena, 11392, N)
    logits = free(arena, 11904, T, E)
    hit = free(arena, 11968, T, 4, E)
    weighed = free(arena, 12224, T, 4, E)
    chosen = free(arena, 12480, T, E)
    gates = free(arena, 12544, T, E + 1)
    place = free(arena, 12610, T, E + 1)
    own = arena[0:E, 12676:12676 + CAP]
    sumsq, rstd = small[:, 0:2], small[:, 2:4]
    top, gate4, first = free(small, 8, T, 8), free(small, 24, T, 4), free(small, 32, T, 8)
    negtop, gsum, most = small[:, 48:50], small[:, 50:52], small[:, 52:53]
    index, flags = M["index"], M["flags"]
    ident, ones, before = const(M, "ident"), const(M, "ones"), const(M, "before")
    numbers = const(M, "slots", ROUNDS, P)
    U, BU, BY, BG = psum[:, 4 * N:6 * N], 4, 6, 7
    UP, DOWN = KC, 4
    W = UP + DOWN

    jobs = Jobs(range(BANKS))
    for t in range(T):
        for half in range(2):
            jobs.add(f"hT{t}{half}", "act" if half else "dve")
    for t in range(T):
        jobs.add(f"lg{t}", "dve")
    for t in range(T):
        jobs.add(f"pl{t}", "dve")
    jobs.add("count", "dve")

    with ctx:
        def sem(name):
            return ctx.enter_context(nc.semaphore("moe_" + name))

        full, freed_by_act, freed_by_dve = sem("full"), sem("freed_by_act"), sem("freed_by_dve")
        freed = {"act": freed_by_act, "dve": freed_by_dve}
        slot_here = [sem(f"slot_here{k}") for k in range(W)]
        slot_used = sem("slot_used")
        row_here, bias_here = sem("row_here"), sem("bias_here")
        step_sem, zero_ready, pads_ready = sem("dve_step"), sem("zero_ready"), sem("pads_ready")
        squares_ready, mean_ready, root_ready, h_ready = sem("squares_ready"), sem("mean_ready"), sem("root_ready"), sem("h_ready")
        negtop_ready, exp_ready, chosen_ready, flags_ready = sem("negtop_ready"), sem("exp_ready"), sem("chosen_ready"), sem("flags_ready")
        own_ready, gated_ready, picked, gathered, xg_ready = sem("own_ready"), sem("gated_ready"), sem("picked"), sem("gathered"), sem("xg_ready")
        glu_ready, sig_ready, a_ready, aT_full, aT_ready = sem("glu_ready"), sem("sig_ready"), sem("a_ready"), sem("aT_full"), sem("aT_ready")
        lin_ready, prod_ready = sem("lin_ready"), sem("prod_ready")
        gatedT_full, gatedT_ready, y_ready, sums_done = sem("gatedT_full"), sem("gatedT_ready"), sem("y_ready"), sem("sums_done")
        block = ctx.enter_context(nc.Block())

        def wait_freed(eng, name):
            job = jobs.by_name[name]
            eng.wait_ge(freed[job.by], job.freed)

        def further_rounds(eng, one_round):
            eng.wait_ge(flags_ready, 1)
            with eng.Fori(1, ROUNDS) as r:
                flag = eng.value_load(flags[0:1, bass.ds(r, 1)], min_val=0, max_val=1)
                with eng.If(flag == 1):
                    one_round(r)
                eng.nop()

        @block.sync
        def _(sp):
            def weights(e):
                for k in range(UP):
                    yield k, ring[:, SLOT * k:SLOT * (k + 1)], A["w_mlp1"][0, bass.ds(e, 1), P * k:P * (k + 1), :].rearrange("o p n -> p (o n)")
                for k in range(DOWN):
                    dst = ring[:, SLOT * (UP + k):SLOT * (UP + k + 1)].rearrange("p (k n) -> p k n", k=2)
                    yield UP + k, dst, A["w_mlp2"][0, bass.ds(e, 1), 2 * P * k:2 * P * (k + 1), :].rearrange("o (k p) n -> p (o k) n", p=P)

            sp.dma_start(M["later"][:, :], A["table_later"]).then_inc(row_here, 16)
            sp.dma_start(wr, A["w_router"][0].rearrange("(k p) e -> p k e", p=P)).then_inc(row_here, 16)
            sp.dma_start(br.unsqueeze(1), A["b_router"][0:1, :].partition_broadcast(P)).then_inc(row_here, 16)
            sp.dma_start(b1, A["b_mlp1"][0]).then_inc(bias_here, 16)
            sp.dma_start(b2, A["b_mlp2"][0]).then_inc(bias_here, 16)
            for k, dst, src in weights(0):
                sp.dma_start(dst, src).then_inc(slot_here[k], 16)

            def experts_from(r, first):
                with sp.Fori(first, E) as e:
                    for k, dst, src in weights(e):
                        sp.wait_ge(slot_used, (r * E + e - 1) * W + k + 1)
                        sp.dma_start(dst, src).then_inc(slot_here[k], 16)

            experts_from(0, 1)
            further_rounds(sp, lambda r: experts_from(r, 0))

        @block.scalar
        def _(act):
            for t in range(T):
                nc.scalar.activation(hn[:, t, :], x_sb[:, t, :], ACT.Square, accum_out=sumsq[:, t:t + 1]).then_inc(squares_ready, 1)
            act.wait_ge(mean_ready, 1)
            nc.scalar.activation(rstd, rstd, ACT.Sqrt).then_inc(root_ready, 1)
            for t in range(T):
                act.wait_ge(full, jobs.full(f"hT{t}1"))
                nc.scalar.copy(actT[:, 4:8, P * t:P * t + P], bank[jobs.by_name[f"hT{t}1"].bank].rearrange("p (k s) -> p k s", k=4)).then_inc(freed_by_act, 1)
            for t in range(T):
                act.wait_ge(negtop_ready, t + 1)
                nc.scalar.activation(gate4[:, t, :], top[:, t, 0:4], ACT.Exp, bias=negtop[:, t:t + 1], accum_out=gsum[:, t:t + 1]).then_inc(exp_ready, 1)
            act.nop().then_inc(aT_ready, 1)
            act.nop().then_inc(y_ready, 1)

            def gather_out(r, e):
                act.wait_ge(gathered, r * (E + 1) + e + 1)
                nc.scalar.copy(xg, bank[BG].rearrange("p (k s) -> p k s", k=KC)).then_inc(xg_ready, 1)

            def one_round(r):
                gather_out(r, 0)
                with act.Fori(0, E) as e:
                    i = r * E + e
                    act.wait_ge(gatedT_full, i + 1)
                    nc.scalar.copy(gatedT, bank[BY][:, 0:T * P].rearrange("p (t s) -> p t s", t=T)).then_inc(gatedT_ready, 1)
                    act.wait_ge(glu_ready, i + 1)
                    nc.scalar.activation(sig, glu, ACT.Sigmoid, scale=SWISH).then_inc(sig_ready, 1)
                    gather_out(r, e + 1)
                    act.wait_ge(aT_full, i + 1)
                    nc.scalar.copy(aT, bank[BU].rearrange("p (k s) -> p k s", k=4)).then_inc(aT_ready, 1)
                    act.wait_ge(slot_used, (i + 1) * W)
                    nc.scalar.copy(y_sb, bank[BY]).then_inc(y_ready, 1)

            one_round(0)
            further_rounds(act, one_round)
        @block.vector
        def _(dve):
            step = Chain(dve, step_sem)
            nc.vector.memset(zeros, 0.0).then_inc(zero_ready, 1)
            step.mark(nc.vector.memset(gates[:, :, E:E + 1], 0.0))
            step.mark(nc.vector.memset(place[:, :, E:E + 1], -1.0))
            dve.wait_ge(squares_ready, T)
            nc.vector.tensor_scalar(rstd, sumsq, 1.0 / D, EPS, ALU.mult, ALU.add).then_inc(mean_ready, 1)
            dve.wait_ge(root_ready, 1)
            step(nc.vector.reciprocal(rstd, rstd))
            for t in range(T):
                step(nc.vector.scalar_tensor_tensor(hn[:, t, :], x_sb[:, t, :], rstd[:, t:t + 1], rows_mod[:, 2, :], ALU.mult, ALU.mult))
                nc.vector.tensor_tensor(hn[:, t, :], hn[:, t, :], rows_mod[:, 1, :], ALU.add).then_inc(h_ready, 1)
            for t in range(T):
                dve.wait_ge(full, jobs.full(f"hT{t}0"))
                nc.vector.tensor_copy(actT[:, 0:4, P * t:P * t + P], bank[jobs.by_name[f"hT{t}0"].bank].rearrange("p (k s) -> p k s", k=4)).then_inc(freed_by_dve, 1)
            dve.wait_ge(row_here, 48)
            for t in range(T):
                dve.wait_ge(full, jobs.full(f"lg{t}"))
                nc.vector.tensor_tensor(logits[:, t, :], bank[jobs.by_name[f"lg{t}"].bank][:, 0:E], br, ALU.add).then_inc(freed_by_dve, 1)
                wait_freed(dve, f"lg{t}")
                step(nc.vector.max(top[:, t, :], logits[:, t, :]))
                nc.vector.tensor_scalar(negtop[:, t:t + 1], top[:, t, 0:1], -1.0, None, ALU.mult).then_inc(negtop_ready, 1)
                step(nc.vector.max_index(index[:, t, :], top[:, t, :], logits[:, t, :]))
                step(nc.vector.tensor_copy(first[:, t, :], index[:, t, :]))
                for j in range(4):
                    step.mark(nc.vector.tensor_scalar(hit[:, t, j, :], numbers[:, 0, 0:E], first[:, t, j:j + 1], None, ALU.is_equal))
                step.sync()
                nc.vector.tensor_reduce(chosen[:, t, :], hit[:, t].rearrange("p j e -> p e j"), AX.X, ALU.add).then_inc(chosen_ready, 1)
            for t in range(T):
                dve.wait_ge(exp_ready, t + 1)
                step(nc.vector.reciprocal(gsum[:, t:t + 1], gsum[:, t:t + 1]))
                for j in range(4):
                    step.mark(nc.vector.tensor_scalar(weighed[:, t, j, :], hit[:, t, j, :], gate4[:, t, j:j + 1], gsum[:, t:t + 1], ALU.mult, ALU.mult))
                step.sync()
                step(nc.vector.tensor_reduce(gates[:, t, 0:E], weighed[:, t].rearrange("p j e -> p e j"), AX.X, ALU.add))
            for t in range(T):
                dve.wait_ge(full, jobs.full(f"pl{t}"))
                dve.wait_ge(chosen_ready, t + 1)
                nc.vector.scalar_tensor_tensor(place[:, t, 0:E], bank[jobs.by_name[f"pl{t}"].bank][:, 0:E], 1.0, chosen[:, t, :], ALU.add, ALU.mult).then_inc(freed_by_dve, 1)
                wait_freed(dve, f"pl{t}")
                step(nc.vector.tensor_scalar(place[:, t, 0:E], place[:, t, 0:E], -1.0, None, ALU.add))
            dve.wait_ge(full, jobs.full("count"))
            nc.vector.tensor_reduce(most, bank[jobs.by_name["count"].bank][:, 0:E], AX.X, ALU.max).then_inc(freed_by_dve, 1)
            wait_freed(dve, "count")
            nc.vector.tensor_scalar(flags[0:1, :], numbers[0:1, :, 0], most[0:1, :], None, ALU.is_lt).then_inc(flags_ready, 1)

            def choose(r, e):
                nc.vector.tensor_tensor(pick, numbers[:, bass.ds(r, 1), 0:CAP].to_broadcast([P, T, CAP]),
                                        place[:, :, bass.ds(e, 1)].to_broadcast([P, T, CAP]), ALU.is_equal).then_inc(picked, 1)

            def one_round(r):
                if not isinstance(r, int):
                    dve.wait_ge(gathered, r * (E + 1))
                choose(r, 0)
                with dve.Fori(0, E) as e:
                    i = r * E + e
                    dve.wait_ge(y_ready, i + 1)
                    nc.vector.tensor_copy(own, ident[0:E, bass.ds(e, 1)].to_broadcast([E, CAP])).then_inc(own_ready, 1)
                    for t in range(T):
                        nc.vector.scalar_tensor_tensor(gated[:, t, :], numbers[:, bass.ds(r, 1), :].rearrange("p o s -> p (o s)"), place[:, t, bass.ds(e, 1)],
                                                       gates[:, t, bass.ds(e, 1)].to_broadcast([P, P]), ALU.is_equal, ALU.mult).then_inc(gated_ready, 1)
                    dve.wait_ge(gathered, r * (E + 1) + e + 1)
                    choose(r, e + 1)
                    dve.wait_ge(slot_used, i * W + UP)
                    both = U.rearrange("p (n two) -> p n two", two=2)
                    nc.vector.tensor_scalar(glu, both[:, :, 0], LIMIT, None, ALU.min).then_inc(glu_ready, 1)
                    nc.vector.tensor_scalar(lin, both[:, :, 1], LIMIT, -LIMIT, ALU.min, ALU.max).then_inc(lin_ready, 1)
                    dve.wait_ge(lin_ready, i + 1)
                    dve.wait_ge(glu_ready, i + 1)
                    nc.vector.scalar_tensor_tensor(lin, lin, 1.0, glu, ALU.add, ALU.mult).then_inc(prod_ready, 1)
                    dve.wait_ge(prod_ready, i + 1)
                    dve.wait_ge(sig_ready, i + 1)
                    nc.vector.tensor_tensor(act_out, lin, sig, ALU.mult).then_inc(a_ready, 1)

            one_round(0)
            further_rounds(dve, one_round)
        @block.tensor
        def _(pe):
            def start(name):
                job = jobs.by_name[name]
                if job.before is not None:
                    pe.wait_ge(freed[job.before.by], job.before.freed)
                return bank[job.bank]

            for t in range(T):
                pe.wait_ge(h_ready, t + 1)
                for half in range(2):
                    b = start(f"hT{t}{half}")
                    for k in range(4):
                        at = N * half + P * k
                        last = nc.tensor.transpose(b[:, P * k:P * k + P], hn[:, t, at:at + P], ident)
                    last.then_inc(full, 1)
            pe.wait_ge(row_here, 48)
            for t in range(T):
                wait_freed(pe, f"hT{t}0")
                wait_freed(pe, f"hT{t}1")
                b = start(f"lg{t}")
                for k in range(KC):
                    last = nc.tensor.matmul(b[:, 0:E], actT[:, k, P * t:P * t + P], wr[:, k, :], start=k == 0, stop=k == KC - 1)
                last.then_inc(full, 1)
            for t in range(T):
                pe.wait_ge(chosen_ready, t + 1)
                b = start(f"pl{t}")
                for j in range(t + 1):
                    last = nc.tensor.matmul(b[:, 0:E], before if j == t else ones, chosen[:, j, :], start=j == 0, stop=j == t)
                last.then_inc(full, 1)
            b = start("count")
            for j in range(T):
                last = nc.tensor.matmul(b[:, 0:E], ones, chosen[:, j, :], start=j == 0, stop=j == T - 1)
            last.then_inc(full, 1)
            wait_freed(pe, "count")
            pe.wait_ge(zero_ready, 1)
            for n in range(4):
                nc.tensor.matmul(bank[n], zeros[:, 0:P], zeros, start=True, stop=False)

            def gather(r, e):
                pe.wait_ge(picked, r * (E + 1) + e + 1)
                for k in range(KC):
                    for t in range(T):
                        last = nc.tensor.matmul(bank[BG][:, CAP * k:CAP * k + CAP], hn[:, t, P * k:P * k + P], pick[:, t, :], start=t == 0, stop=t == T - 1)
                last.then_inc(gathered, 1)

            def one_round(r):
                if not isinstance(r, int):
                    pe.wait_ge(xg_ready, r * (E + 1))
                gather(r, 0)
                with pe.Fori(0, E) as e:
                    i = r * E + e
                    pe.wait_ge(xg_ready, r * (E + 1) + e + 1)
                    pe.wait_ge(own_ready, i + 1)
                    pe.wait_ge(aT_ready, i + 1)
                    for n in range(2):
                        for h in range(2):
                            nc.tensor.matmul(U[CAP * h:CAP * h + CAP, N * n:N * n + N], own, b1[:, 2 * N * h + N * n:2 * N * h + N * n + N], start=True, stop=False)
                    for k in range(UP):
                        pe.wait_ge(slot_here[k], (i + 1) * 16)
                        for n in range(2):
                            for h in range(2):
                                at = SLOT * k + 2 * N * h + N * n
                                last = nc.tensor.matmul(U[CAP * h:CAP * h + CAP, N * n:N * n + N], xg[:, k, :], ring[:, at:at + N], start=False, stop=k == UP - 1)
                        last.then_inc(slot_used, 1)
                    pe.wait_ge(gated_ready, (i + 1) * T)
                    for t in range(T):
                        last = nc.tensor.transpose(bank[BY][:, P * t:P * t + P], gated[:, t, :], ident)
                    last.then_inc(gatedT_full, 1)
                    gather(r, e + 1)
                    pe.wait_ge(a_ready, i + 1)
                    for k in range(4):
                        last = nc.tensor.transpose(bank[BU][:, P * k:P * k + P], act_out[:, P * k:P * k + P], ident)
                    last.then_inc(aT_full, 1)
                    pe.wait_ge(gatedT_ready, i + 1)
                    for h in range(2):
                        nc.tensor.matmul(bank[BY][CAP * h:CAP * h + CAP, :], own, b2[:, N * h:N * h + N], start=True, stop=False)
                    pe.wait_ge(aT_ready, i + 2)
                    for k in range(KC):
                        if k % 2 == 0:
                            pe.wait_ge(slot_here[UP + k // 2], (i + 1) * 16)
                        for h in range(2):
                            at = SLOT * UP + D * k + N * h
                            last = nc.tensor.matmul(bank[BY][CAP * h:CAP * h + CAP, :], aT[:, k % 4, CAP * (k // 4):CAP * (k // 4) + CAP], ring[:, at:at + N], start=False, stop=k == KC - 1)
                        if k % 2:
                            last.then_inc(slot_used, 1)
                    pe.wait_ge(y_ready, i + 2)
                    for t in range(T):
                        for h in range(2):
                            nc.tensor.matmul(bank[2 * t + h], gatedT[CAP * h:CAP * h + CAP, t, :], y_sb[CAP * h:CAP * h + CAP, :], start=False, stop=False)

            pe.wait_ge(bias_here, 32)
            one_round(0)
            further_rounds(pe, one_round)
            for n in range(4):
                last = nc.tensor.matmul(bank[n], zeros[:, 0:P], zeros, start=False, stop=True)
            last.then_inc(sums_done, 1)
            pe.wait_ge(sums_done, 1)


def layer(nc, M, A, i, out=None):
    x_sb, bank, small = M["x"], M["bank"], M["small"]
    ctx = ExitStack()
    RING_LAYER = 4
    QK = W_MIX // P
    CAT, HID, MEM = KC, KC, 2 * KC
    arena = ctx.enter_context(nc.sbuf_tensor(f"layer{i}_arena", [P, 9728], FP32))
    ring = ctx.enter_context(nc.sbuf_tensor(f"layer{i}_ring", [P, RING_LAYER * SLOT], FP32))
    high = ctx.enter_context(nc.sbuf_tensor(f"layer{i}_w_hi", [P, BUFFERS, UNIT], F32R))
    low = ctx.enter_context(nc.sbuf_tensor(f"layer{i}_w_lo", [P, BUFFERS, UNIT], F32R))
    xh = ctx.enter_context(nc.sbuf_tensor(f"layer{i}_x_hi", [P, HID + FC2, S], F32R))
    xl = ctx.enter_context(nc.sbuf_tensor(f"layer{i}_x_lo", [P, HID + FC2, S], F32R))
    rows = free(M["base"], 0, 4, D)
    kmT, vm = free(M["kv"], 1024 * i, 2, N_MEM), free(M["kv"], 1024 * i + 512, 2, W_MEM)
    u_nat, wsT, v_nat, v_rows = free(arena, 0, T, W_MIX), free(arena, 1536, HEADS, P), free(arena, 3072, T, W_MIX), free(arena, 4608, 2, W_MIX)
    mem_nat = free(arena, 0, T, D)
    qT, kT, v_self = free(arena, 0, QK, S), free(arena, 1536, QK, S), free(arena, 3072, T, W_MIX)
    silu, hid = free(arena, 0, 2, N), free(arena, 1024, 2, N)
    probs = free(arena, 6144, 2, 4, S)
    ws = free(arena, 6144, HEADS, P)
    probsT = free(arena, 8192, 2, 4, P)
    g_fin = free(arena, 8192, D)
    qmT = free(arena, 9216, 2, S)
    stats, mv, root = free(small, 0, T, 3, 6), free(small, 36, T, 2), small[:, 40:42]
    bsT, negmax, lsum = small[:, 44:56], free(small, 56, 2, 4), free(small, 64, 2, 4)
    sumsq, rstd = small[:, 72:74], small[:, 74:76]
    bs = M["b12"][:, 0:P]
    ident, upto, causal = const(M, "ident"), const(M, "upto"), const(M, "causal")

    jobs = Jobs(range(BANKS))
    w_kv, w_in = A["w_mem_kv_2"], A["b_w_in_2" if i else "a_w_in_2"][0]
    units = [("mem", 0, t) for t in range(T)]
    if i:
        units += [("self", c, t) for c in range(3) for t in range(T)]

    def scores(u):
        by = "act" if units[u][0] == "mem" else "dve"
        jobs.add(f"sa{u}", by)
        jobs.add(f"sb{u}", by)

    def weights_over(u):
        kind, c, t = units[u]
        for n in range(2 if kind == "mem" else t + 1):
            jobs.add(f"pT{u}:{n}", "act")

    def transposes(name):
        for t in range(T):
            for half in range(2):
                jobs.add(f"{name}{t}{half}", "dve", high=True)

    if i == 0:
        jobs.banks = list(range(BANKS // 2, BANKS))
        transposes("memT")
        for n in range(DEPTH_2):
            jobs.add(f"km{n}", "act", jobs.wide(w_kv[n], 0))
            jobs.pair(f"vm{n}", "act", jobs.rows(w_kv[n], W_MEM, W_MEM))
        jobs.banks, jobs.turn = list(range(BANKS)), 0
        transposes("xT")
        for n in range(3):
            jobs.add(f"wsT{n}", "dve")
        jobs.add("bsT", "dve")
        jobs.pair("vn0", "act", jobs.rows(w_in, W_MIX))
        jobs.add("qm", "act", jobs.wide(w_in, 2 * W_MIX))
        jobs.pair("vn1", "act", jobs.rows(w_in, W_MIX + N, W_MIX - N))
        scores(0)
        jobs.pair("un0", "act", jobs.rows(w_in, 0))
        weights_over(0)
        scores(1)
        jobs.add("ao0", "dve", high=True)
        jobs.pair("un1", "act", jobs.rows(w_in, N, W_MIX - N))
        weights_over(1)
        jobs.add("sv0", "dve")
        jobs.add("ao1", "dve", high=True)
        for n in range(1, 3):
            jobs.add(f"sv{n}", "dve")
        for n in range(3):
            jobs.add(f"mixT{n}", "dve", high=True)
    else:
        transposes("xT")
        jobs.add("qm", "act", jobs.wide(w_in, 3 * W_MIX))
        fill = [(f"{what}{n}", at + WIDE * n) for n in range(3) for what, at in (("q_", 0), ("k_", W_MIX), ("v_", 2 * W_MIX))]

        def some():
            if fill:
                name, col = fill.pop(0)
                if name[0] == "v":
                    jobs.pair(name, "act", jobs.rows(w_in, col, WIDE))
                else:
                    jobs.add(name, "act", jobs.wide(w_in, col))

        some()
        for u in range(len(units) + 1):
            if u:
                weights_over(u - 1)
            if u < len(units):
                scores(u)
            if u:
                jobs.add(f"ao{u - 1}", "dve", high=True)
            some()
            if u == len(units) - 3:
                some()
        assert not fill
    for half in range(2):
        jobs.pair(f"pr{half}", "dve", jobs.rows(A["w_mix_out_2"][i], N * half), apart=half == 1)
    transposes("yT")
    w_ffn = A["w_ffn_in_2"][i]
    for n in range(F2 // WIDE):
        jobs.add(f"fg{n}", "act", jobs.wide(w_ffn, WIDE * n))
        jobs.add(f"fu{n}", "dve", jobs.wide(w_ffn, F2 + WIDE * n))
    for half in range(2):
        jobs.pair(f"fo{half}", "dve", jobs.rows(A["w_ffn_out_2"][i], N * half), apart=half == 1)

    with ctx:
        def sem(name):
            return ctx.enter_context(nc.semaphore(f"layer{i}_{name}"))

        stream = Stream(nc, sem, jobs, ring, RING_LAYER, high, low)
        full, freed_by_act, freed_by_dve, wait_freed = stream.full, stream.freed["act"], stream.freed["dve"], stream.wait_freed
        xh_ready, hid_high, hid_low = sem("xh_ready"), sem("hid_high"), sem("hid_low")
        fin_here, sums_taken, squares_ready, mean_ready, fin_root_ready, fin_ready = (
            sem("fin_here"), sem("sums_taken"), sem("squares_ready"), sem("mean_ready"), sem("fin_root_ready"), sem("fin_ready"))
        rows_here, mem_here, ws_here, v_rows_here, bs_here = sem("rows_here"), sem("mem_here"), sem("ws_here"), sem("v_rows_here"), sem("bs_here")
        step_sem, var_ready, root_ready, v_ready, x_sums_ready = sem("dve_step"), sem("var_ready"), sem("root_ready"), sem("v_ready"), sem("x_sums_ready")
        squares = free(arena, 6144, T, D)
        max_ready, exp_ready, probs_ready, x_ready, out_done = sem("max_ready"), sem("exp_ready"), sem("probs_ready"), sem("x_ready"), sem("out_done")
        block = ctx.enter_context(nc.Block())

        def two_parts(job, b, parts):
            name = job.name
            if name.startswith("ao"):
                kind, c, t = units[int(name[2:])]
                at = CAT + (QK if kind == "mem" else 2 * c)
                return parts[:, at:at + 2, P * t:P * t + P], b[:, 0:2 * P].rearrange("p (a s) -> p a s", a=2)
            if name.startswith("mixT"):
                at = CAT + 2 * int(name[4])
                return parts[:, at:at + 2, :], b.rearrange("p (a s) -> p a s", a=2)
            t, half = int(name[-2]), int(name[-1])
            at = 4 * half + (MEM if name[0] == "m" else 0)
            return parts[:, at:at + 4, P * t:P * t + P], b.rearrange("p (k s) -> p k s", k=4)

        @block.sync
        def _(sp):
            if i == 0:
                sp.dma_start(mem_nat, A["mem_2"][0].rearrange("(t p) d -> p t d", p=P)).then_inc(mem_here, 16)
                sp.dma_start(bs, A["a_b_s_2"][0]).then_inc(bs_here, 16)
            for q in range(len(jobs.slots)):
                stream.load(sp, q)
                if i == 0 and q == 1:
                    sp.dma_start(g_fin.unsqueeze(1), A["g_final"].rearrange("(o d) -> o d", o=1).partition_broadcast(P)).then_inc(fin_here, 16)
            if out is not None:
                for t in range(T):
                    sp.wait_ge(x_ready, T + t + 1)
                    sp.dma_start(out[0, P * t:P * t + P, :], x_sb[:, t, :]).then_inc(out_done, 16)
                sp.wait_ge(out_done, 16 * T)

        @block.gpsimd
        def _(pool):
            if i == 0:
                for n, name in enumerate(("a_ln_v_g_2", "a_ln_v_b_2")):
                    pool.dma_start(v_rows[:, n, :].unsqueeze(1), A[name][0:1, :].partition_broadcast(P)).then_inc(v_rows_here, 16)
                pool.wait_ge(sums_taken, 2 * T)
                pool.wait_ge(squares_ready, T)
                pool.dma_start(ws, A["a_w_s_2"][0].rearrange("g t s -> t g s")).then_inc(ws_here, 16)
            for n, name in enumerate(("ln_mix_g_2", "ln_mix_b_2", "ln_ffn_g_2", "ln_ffn_b_2")):
                pool.dma_start(rows[:, n, :].unsqueeze(1), A[name][i:i + 1, :].partition_broadcast(P)).then_inc(rows_here, 16)
            pool.wait_ge(rows_here, 64)

        @block.scalar
        def _(act):
            roots = [0]

            def take_root(t):
                roots[0] += 1
                act.wait_ge(var_ready, roots[0])
                nc.scalar.activation(root[:, t:t + 1], mv[:, t, 1:2], ACT.Sqrt).then_inc(root_ready, 1)

            def final_roots():
                for t in range(T):
                    act.wait_ge(x_sums_ready, 2 * (t + 1))
                    nc.scalar.activation(squares[:, t, :], x_sb[:, t, :], ACT.Square, accum_out=sumsq[:, t:t + 1]).then_inc(squares_ready, 1)
                act.wait_ge(mean_ready, 1)
                nc.scalar.activation(rstd, rstd, ACT.Sqrt).then_inc(fin_root_ready, 1)

            for what, job in jobs.sequence():
                if what == "split":
                    stream.split_high(act, job)
                    continue
                name, b = job.name, bank[job.bank]
                pair = b.rearrange("p (a s) -> p a s", a=2)
                if name == "vm0t0" and i == 0:
                    final_roots()
                if job.hi:
                    act.wait_ge(full, job.index + 1)
                    dst, src = two_parts(job, b, xh)
                    nc.scalar.copy(dst, src).then_inc(xh_ready, 1)
                    continue
                if name.startswith("fu"):
                    n = int(name[2:])
                    wait_freed(act, name)
                    nc.scalar.copy(xh[:, HID + 2 * n:HID + 2 * n + 2, :], hid[:, n % 2, :].rearrange("p (a s) -> p a s", a=2)).then_inc(hid_high, 1)
                    continue
                if name[:2] in ("sa", "sb"):
                    u, part = int(name[2:]), "ab".index(name[1])
                    kind, c, t = units[u]
                    w = S if kind == "mem" else P * (t + 1)
                    act.wait_ge(max_ready, 2 * u + part + 1)
                    for n in range(2):
                        at = 2 * part + n
                        dst = probs[:, u % 2, at, 0:w]
                        last = nc.scalar.activation(dst, pair[:, n, :] if kind == "mem" else dst, ACT.Exp, bias=negmax[:, u % 2, at:at + 1], accum_out=lsum[:, u % 2, at:at + 1])
                        if n == 1 and kind == "mem":
                            last.then_inc(freed_by_act, 1)
                        elif n == 1:
                            last.then_inc(exp_ready, 1)
                    if name == "sb0" and i == 0:
                        for tile in range(T):
                            take_root(tile)
                    continue
                if job.by != "act":
                    if name.startswith("pr1t") or name.startswith("fo1t"):
                        take_root(int(name[4]))
                    continue
                act.wait_ge(full, job.index + 1)
                if name[:2] in ("vn", "un"):
                    n, t = int(name[2]), int(name[4])
                    w = W_MIX - N if n else N
                    dst = v_nat if name[0] == "v" else u_nat
                    last = nc.scalar.activation(dst[:, t, N * n:N * n + w], b[:, 0:w], ACT.Gelu_apprx_tanh)
                elif name == "qm":
                    last = nc.scalar.mul(qmT, pair, DH ** -0.5)
                elif name.startswith("km"):
                    last = nc.scalar.copy(free(M["kv"], 1024 * int(name[2]), 2, N_MEM), pair)
                elif name.startswith("vm"):
                    last = nc.scalar.copy(free(M["kv"], 1024 * int(name[2]) + 512, 2, W_MEM)[:, int(name[4]), :], b[:, 0:W_MEM])
                elif name.startswith("q_"):
                    n = int(name[2])
                    last = nc.scalar.mul(qT[:, 2 * n:2 * n + 2, :], pair, DH ** -0.5)
                elif name.startswith("k_"):
                    n = int(name[2])
                    last = nc.scalar.copy(kT[:, 2 * n:2 * n + 2, :], pair)
                elif name.startswith("v_"):
                    n, t = int(name[2]), int(name[4])
                    last = nc.scalar.copy(v_self[:, t, WIDE * n:WIDE * n + WIDE], b[:, 0:WIDE])
                elif name.startswith("pT"):
                    n = int(name.split(":")[1])
                    last = nc.scalar.copy(probsT[:, n], b.rearrange("p (h s) -> p h s", h=4))
                elif name.startswith("fg"):
                    n = int(name[2:])
                    if n >= 2:
                        wait_freed(act, f"fu{n - 2}")
                    last = nc.scalar.activation(silu[:, n % 2, :], b, ACT.Silu)
                last.then_inc(freed_by_act, 1)

        @block.vector
        def _(dve):
            step = Chain(dve, step_sem)
            roots = [0]

            def take_sums():
                for t in range(T):
                    for half in range(2):
                        cols = slice(N * half, N * half + N)
                        nc.vector.tensor_tensor(squares[:, t, cols], bank[2 * t + half], rows[:, 3, cols], ALU.mult).then_inc(sums_taken, 1)
                        dve.wait_ge(sums_taken, 2 * t + half + 1)
                        nc.vector.tensor_tensor(x_sb[:, t, cols], x_sb[:, t, cols], squares[:, t, cols], ALU.add).then_inc(x_sums_ready, 1)

            def final_norm():
                dve.wait_ge(squares_ready, T)
                nc.vector.tensor_scalar(rstd, sumsq, 1.0 / D, EPS, ALU.mult, ALU.add).then_inc(mean_ready, 1)
                dve.wait_ge(fin_root_ready, 1)
                step(nc.vector.reciprocal(rstd, rstd))
                dve.wait_ge(fin_here, 16)
                for t in range(T):
                    nc.vector.scalar_tensor_tensor(x_sb[:, t, :], x_sb[:, t, :], rstd[:, t:t + 1], g_fin, ALU.mult, ALU.mult).then_inc(fin_ready, 1)

            def norm(t, pieces, v, g, b, ready):
                step(nc.vector.bn_aggr(mv[:, t, :], stats[:, t, 0:pieces, :]))
                nc.vector.tensor_scalar(mv[:, t, 1:2], mv[:, t, 1:2], LN_EPS, None, ALU.add).then_inc(var_ready, 1)
                step.mark(nc.vector.scalar_tensor_tensor(v, v, mv[:, t, 0:1], g, ALU.subtract, ALU.mult))
                roots[0] += 1
                dve.wait_ge(root_ready, roots[0])
                step(nc.vector.reciprocal(root[:, t:t + 1], root[:, t:t + 1]))
                nc.vector.scalar_tensor_tensor(v, v, root[:, t:t + 1], b, ALU.mult, ALU.add).then_inc(ready, 1)

            def divide(u):
                kind, c, t = units[u]
                w = S if kind == "mem" else P * (t + 1)
                if kind == "mem":
                    wait_freed(dve, f"sb{u}")
                else:
                    dve.wait_ge(exp_ready, 2 * (u - T) + 2)
                step(nc.vector.reciprocal(lsum[:, u % 2, :], lsum[:, u % 2, :]))
                pr = probs[:, u % 2, :, 0:w]
                nc.vector.tensor_tensor(pr, pr, lsum[:, u % 2, :].unsqueeze(2).to_broadcast([P, 4, w]), ALU.mult).then_inc(probs_ready, 1)

            def hidden_low(n):
                wait_freed(dve, f"fu{n}")
                dve.wait_ge(hid_high, n + 1)
                places = (slice(None), slice(HID + 2 * n, HID + 2 * n + 2), slice(None))
                nc.vector.tensor_tensor(xl[places], hid[:, n % 2, :].rearrange("p (a s) -> p a s", a=2), xh[places].bitcast(FP32), ALU.subtract).then_inc(hid_low, 1)

            for what, job in jobs.sequence():
                if what == "split":
                    stream.split_low(dve, job)
                    continue
                name, b = job.name, bank[job.bank]
                pair = b.rearrange("p (a s) -> p a s", a=2)
                if name == "km0":
                    take_sums()
                if name == "vm0t1":
                    final_norm()
                if name == "pr0t0":
                    dve.wait_ge(rows_here, 64)
                if job.hi:
                    dve.wait_ge(full, job.index + 1)
                    dve.wait_ge(xh_ready, job.hi)
                    dst, src = two_parts(job, b, xl)
                    nc.vector.tensor_tensor(dst, src, two_parts(job, b, xh)[0].bitcast(FP32), ALU.subtract).then_inc(freed_by_dve, 1)
                    if name[:2] == "ao" and int(name[2:]) + 1 < len(units):
                        divide(int(name[2:]) + 1)
                    continue
                if name.startswith("vn"):
                    n, t = int(name[2]), int(name[4])
                    wait_freed(dve, name)
                    step.mark(nc.vector.bn_stats(stats[:, t, n, :], v_nat[:, t, N * n:min(N * n + N, W_MIX)]))
                    continue
                if name[:2] in ("sa", "sb"):
                    u, part = int(name[2:]), "ab".index(name[1])
                    kind, c, t = units[u]
                    dve.wait_ge(full, job.index + 1)
                    src = pair
                    if kind == "self":
                        w = P * (t + 1)
                        src = probs[:, u % 2, 2 * part:2 * part + 2, 0:w]
                        mask = causal[:, S - w:S].unsqueeze(1).to_broadcast([P, 2, w])
                        nc.vector.tensor_tensor(src, pair[:, :, 0:w], mask, ALU.add).then_inc(freed_by_dve, 1)
                        dve.wait_ge(freed_by_dve, job.freed)
                    nc.vector.tensor_reduce(negmax[:, u % 2, 2 * part:2 * part + 2], src, AX.X, ALU.max, negate=True).then_inc(max_ready, 1)
                    if name == "sb0":
                        divide(0)
                    if name == "sb0" and i == 0:
                        step.sync()
                        dve.wait_ge(v_rows_here, 32)
                        for tile in range(T):
                            norm(tile, 2, v_nat[:, tile, :], v_rows[:, 0, :], v_rows[:, 1, :], v_ready)
                    continue
                if job.by != "dve":
                    continue
                dve.wait_ge(full, job.index + 1)
                if name.startswith("wsT"):
                    n = int(name[3])
                    nc.vector.tensor_tensor(wsT[:, 4 * n:4 * n + 4, :], b.rearrange("p (g s) -> p g s", g=4), upto.unsqueeze(1).to_broadcast([P, 4, P]), ALU.mult).then_inc(freed_by_dve, 1)
                elif name == "bsT":
                    nc.vector.tensor_copy(bsT, b[:, 0:HEADS]).then_inc(freed_by_dve, 1)
                elif name.startswith("sv"):
                    n = int(name[2])
                    wait_freed(dve, "bsT")
                    wait_freed(dve, "un1t1")
                    for j in range(4):
                        g = 4 * n + j
                        cols = u_nat[:, :, DH * g:DH * g + DH]
                        last = nc.vector.scalar_tensor_tensor(cols, b.rearrange("p (g c d) -> p g c d", g=4, c=T)[:, j], bsT[:, g:g + 1], cols, ALU.add, ALU.mult)
                    last.then_inc(freed_by_dve, 1)
                elif name[:2] in ("pr", "fo"):
                    half, t = int(name[2]), int(name[4])
                    cols = x_sb[:, t, N * half:N * half + N]
                    nc.vector.scalar_tensor_tensor(cols, cols, ALPHA, b, ALU.mult, ALU.add).then_inc(freed_by_dve, 1)
                    dve.wait_ge(freed_by_dve, job.freed)
                    step.mark(nc.vector.bn_stats(stats[:, t, half, :], cols))
                    if half:
                        step.sync()
                        r = 0 if name[0] == "p" else 2
                        norm(t, 2, x_sb[:, t, :], rows[:, r, :], rows[:, r + 1, :], x_ready)
                elif name.startswith("fu"):
                    n = int(name[2:])
                    wait_freed(dve, f"fg{n}")
                    if n >= 2:
                        dve.wait_ge(hid_low, n - 1)
                    nc.vector.tensor_tensor(hid[:, n % 2, :], silu[:, n % 2, :], b, ALU.mult).then_inc(freed_by_dve, 1)
                    if n:
                        hidden_low(n - 1)
                    if n == F2 // WIDE - 1:
                        hidden_low(n)

        @block.tensor
        def _(pe):
            def pair_of(job, at, ready=None):
                other = jobs.by_name[job.name[:-1] + "1"]
                stream.start(pe, other)
                stream.natural(pe, (job, other), [bank[j.bank][:, 0:jobs.slots[j.slots[0]][1].shape[2]] for j in (job, other)], xh[:, at:, :], xl[:, at:, :], ready)

            for job in jobs.list:
                name, b = job.name, bank[job.bank]
                if job.units and name[-2:] == "t1":
                    continue
                stream.start(pe, job)
                if job.before is None and job.bank < BANKS // 2 and i == 0:
                    pe.wait_ge(sums_taken, 2 * T)
                if name[:2] in ("xT", "yT"):
                    t, half = int(name[2]), int(name[3])
                    if name[0] == "y":
                        pe.wait_ge(x_ready, t + 1)
                    elif i == 0:
                        pe.wait_ge(fin_ready, t + 1)
                    for k in range(4):
                        at = N * half + P * k
                        last = nc.tensor.transpose(b[:, P * k:P * k + P], x_sb[:, t, at:at + P], ident)
                elif name.startswith("memT"):
                    t, half = int(name[4]), int(name[5])
                    pe.wait_ge(mem_here, 16)
                    for k in range(4):
                        at = N * half + P * k
                        last = nc.tensor.transpose(b[:, P * k:P * k + P], mem_nat[:, t, at:at + P], ident)
                elif name[:2] in ("vn", "un", "v_"):
                    wait_freed(pe, "xT11")
                    pair_of(job, 0)
                    continue
                elif name[:2] in ("q_", "k_", "qm"):
                    wait_freed(pe, "xT11")
                    stream.transposed(pe, job, b, xh, xl)
                    continue
                elif name.startswith("km"):
                    wait_freed(pe, "memT11")
                    stream.transposed(pe, job, b, xh[:, MEM:MEM + KC, :], xl[:, MEM:MEM + KC, :])
                    continue
                elif name.startswith("vm"):
                    pair_of(job, MEM)
                    continue
                elif name.startswith("wsT"):
                    n = int(name[3])
                    pe.wait_ge(ws_here, 16)
                    for j in range(4):
                        last = nc.tensor.transpose(b[:, P * j:P * j + P], ws[:, 4 * n + j, :], ident)
                elif name == "bsT":
                    pe.wait_ge(bs_here, 16)
                    last = nc.tensor.transpose(b[:, 0:HEADS], bs, ident[0:HEADS, 0:HEADS])
                elif name[:2] in ("sa", "sb"):
                    u, part = int(name[2:]), "ab".index(name[1])
                    kind, c, t = units[u]
                    q_, k_, at, w = (qmT, kmT, 0, S) if kind == "mem" else (qT, kT, 2 * c, P * (t + 1))
                    wait_freed(pe, "qm" if kind == "mem" else f"k_{c}")
                    r = slice(DH * part, DH * part + DH)
                    for n in range(2):
                        last = nc.tensor.matmul(b[:, S * n:S * n + w], q_[r, at + n, P * t:P * t + P], k_[r, at + n, 0:w], start=True, stop=True)
                elif name.startswith("pT"):
                    u, n = (int(v) for v in name[2:].split(":"))
                    pe.wait_ge(probs_ready, u + 1)
                    for h in range(4):
                        last = nc.tensor.transpose(b[:, P * h:P * h + P], probs[:, u % 2, h, P * n:P * n + P], ident)
                elif name.startswith("ao"):
                    u = int(name[2:])
                    kind, c, t = units[u]
                    blocks = 2 if kind == "mem" else t + 1
                    wait_freed(pe, f"pT{u}:{blocks - 1}")
                    if kind == "self":
                        wait_freed(pe, f"v_{c}t1")
                    v = vm if kind == "mem" else v_self
                    for n in range(2):
                        for part in range(2):
                            for m in range(blocks):
                                at = (0 if kind == "mem" else 4 * c * DH) + DH * (2 * n + part)
                                last = nc.tensor.matmul(b[DH * part:DH * part + DH, P * n:P * n + P], v[:, m, at:at + DH], probsT[:, m, 2 * part + n, :],
                                                        start=m == 0, stop=m == blocks - 1)
                elif name.startswith("sv"):
                    n = int(name[2])
                    pe.wait_ge(v_ready, T)
                    wait_freed(pe, f"wsT{n}")
                    for j in range(4):
                        g = 4 * n + j
                        last = nc.tensor.matmul(b[:, T * DH * j:T * DH * (j + 1)], wsT[:, g, :], v_nat[:, :, DH * g:DH * g + DH], start=True, stop=True)
                elif name.startswith("mixT"):
                    n = int(name[4])
                    wait_freed(pe, f"sv{n}")
                    for a in range(2):
                        for t in range(T):
                            last = nc.tensor.transpose(b[:, S * a + P * t:S * a + P * t + P], u_nat[:, t, P * (2 * n + a):P * (2 * n + a) + P], ident)
                elif name[:2] in ("fg", "fu"):
                    wait_freed(pe, "yT11")
                    stream.transposed(pe, job, b, xh, xl)
                    continue
                elif name.startswith("pr"):
                    wait_freed(pe, f"ao{len(units) - 1}")
                    if i == 0:
                        wait_freed(pe, "mixT2")
                    pair_of(job, CAT)
                    continue
                elif name.startswith("fo"):
                    pair_of(job, HID, lambda n: pe.wait_ge(hid_low, n + 1))
                    continue
                last.then_inc(full, 1)


def layers(nc, M, A, out):
    layer(nc, M, A, 0)
    layer(nc, M, A, 1, out)


def program(nc, A, out):
    scratch = nc.dram_tensor("bias_by_distance", (AG * AH, TAB), FP32, kind="Internal").ap()
    with ExitStack() as ctx:
        def sb(name, shape, dt=FP32):
            return ctx.enter_context(nc.sbuf_tensor(name, shape, dt))

        psum = ctx.enter_context(nc.psum_tensor("psum", [P, BANKS * N], FP32))
        M = {
            "psum": psum,
            "bank": [psum[:, N * n:N * n + N] for n in range(BANKS)],
            "x": sb("x_res", [P, T, D]),
            "base": sb("base", [P, 4 * D]),
            "common": sb("common_consts", [P, TABLE_W["common"]]),
            "small": sb("small", [P, 384]),
            "b12": sb("b12", [12, N]),
            "mv8": sb("mv8", [P, RH * T, 2])[:, :, :],
            "var8": sb("var8", [P, RH * T])[:, :],
            "index": sb("index", [P, T, 8], mybir.dt.uint32),
            "flags": sb("flags", [1, ROUNDS], I32),
        }
        mixer(nc, M, A, scratch)
        M["later"] = sb("later_consts", [P, TABLE_W["later"]])
        M["kv"] = sb("memory_kv", [P, DEPTH_2 * 1024])
        experts(nc, M, A)
        layers(nc, M, A, out)


def kernel(**inputs):
    import numpy as _np
    import concourse.bacc as _bacc
    from concourse import mybir as _mybir
    from concourse.bass_utils import run_bass_kernel_spmd as _run

    nc = _bacc.Bacc("TRN2", target_bir_lowering=False, num_devices=1)
    arrays, A = {}, {}
    tables, onehot = shape_constants()
    for name, a in [*inputs.items(), *(("table_" + n, a) for n, a in tables.items()), ("onehot", onehot)]:
        a = _np.ascontiguousarray(a)
        arrays[f"in_{name}_dram"] = a
        A[name] = nc.dram_tensor(f"in_{name}_dram", a.shape, _mybir.dt.from_np(a.dtype), kind="ExternalInput").ap()
    out = nc.dram_tensor("out_dram", (1, S, D), FP32, kind="ExternalOutput").ap()
    program(nc, A, out)
    r = _run(nc, [arrays], core_ids=[0])
    return r.results[0]["out_dram"]
```
